# Optimizing a Trainium2 kernel written in Bass

```python
import jax
import jax.numpy as jnp
from jax import lax
import numpy as np

D_MODEL = 1024
BATCH = 1
SEQ = 512
DEPTH = 1
DEC_BATCH = 8
DEC_SEQ = 4
PAST_LEN = 1024
PAGE_SIZE = 128

HEAD_DIM = 64
MIX_WIDTH = D_MODEL
ATTN_HEADS = 8
KV_HEADS = 2
GROUP = ATTN_HEADS // KV_HEADS
ATTN_WIDTH = ATTN_HEADS * HEAD_DIM
KV_WIDTH = KV_HEADS * HEAD_DIM
N_BRANCH = 3
BLOCK_CMP = 32
STRIDE_CMP = 16
CMP_RATIO = BLOCK_CMP // STRIDE_CMP
CMP_HIDDEN = 2 * HEAD_DIM
SEL_BLOCK = 64
TOP_BLOCKS = 16
WINDOW = 512
Q_BLOCK = 128
POOL_WIDTH = MIX_WIDTH - ATTN_WIDTH
POOL_WINDOWS = (2, 4, 8, 16)
POOL_GROUPS = len(POOL_WINDOWS)
POOL_GROUP_WIDTH = POOL_WIDTH // POOL_GROUPS
POOL_MAX = max(POOL_WINDOWS)
POOL_STATE = POOL_MAX - 1
IN_COLS = ATTN_WIDTH + 2 * N_BRANCH * KV_WIDTH + N_BRANCH * ATTN_HEADS + POOL_WIDTH
PEER_HEADS = 8
N_KEYS = 128
N_EXPERTS = N_KEYS * N_KEYS
D_KEY = 256
PEER_TOPK = 16
PEER_BLOCK = 128
ALIBI_MAX_BIAS = 8.0
RMS_EPS = 1e-6
NEG_INF = -1e30
FORCE_BONUS = 1e4
SCALE = HEAD_DIM ** -0.5

kernel_name = 'nsa_pool_peer_hybrid_step'

def rmsnorm(x, g):
    xf = x.astype(jnp.float32)
    y = xf * lax.rsqrt(jnp.mean(xf * xf, axis=-1, keepdims=True) + RMS_EPS)
    return (y * g.astype(jnp.float32)).astype(x.dtype)

def masked_softmax(s, mask, axis=-1):
    p = jax.nn.softmax(jnp.where(mask, s, NEG_INF), axis=axis)
    return jnp.where(mask, p, 0.0)

def alibi_slopes():
    h = jnp.arange(1, ATTN_HEADS + 1, dtype=jnp.float32)
    return (2.0 ** (-ALIBI_MAX_BIAS * h / ATTN_HEADS)).reshape(KV_HEADS, GROUP)

def project(x, norm1_g, w_in, q_norm_g, k_norm_g):
    B, T, _ = x.shape
    z = jnp.einsum('btd,dc->btc', rmsnorm(x, norm1_g), w_in)
    o1 = ATTN_WIDTH
    o2 = o1 + 2 * N_BRANCH * KV_WIDTH
    o3 = o2 + N_BRANCH * ATTN_HEADS
    q = rmsnorm(z[..., :o1].reshape(B, T, KV_HEADS, GROUP, HEAD_DIM), q_norm_g)
    kv = z[..., o1:o2].reshape(B, T, N_BRANCH, 2, KV_HEADS, HEAD_DIM)
    gates = jax.nn.sigmoid(z[..., o2:o3].astype(jnp.float32)).reshape(B, T, N_BRANCH, KV_HEADS, GROUP)
    u_pool = z[..., o3:]
    cmp_rows = kv[:, :, 0]
    sel_rows = jnp.stack([rmsnorm(kv[:, :, 1, 0], k_norm_g[1]), kv[:, :, 1, 1]], axis=2)
    win_rows = jnp.stack([rmsnorm(kv[:, :, 2, 0], k_norm_g[2]), kv[:, :, 2, 1]], axis=2)
    return q, gates, cmp_rows, sel_rows, win_rows, u_pool

def sub_proj(rows, cmp_w1):
    B, L = rows.shape[:2]
    n_sub = L // STRIDE_CMP
    sub = rows[:, :n_sub * STRIDE_CMP].reshape(B, n_sub, STRIDE_CMP, 2, KV_HEADS, HEAD_DIM)
    w1 = cmp_w1.reshape(2, CMP_RATIO, STRIDE_CMP, HEAD_DIM, CMP_HIDDEN)
    return jnp.einsum('bnscgd,crsde->bnrcge', sub, w1)

def compress(sub, k_norm_g, cmp_pos, cmp_w1, cmp_w2):
    n_cmp = sub.shape[1] - CMP_RATIO + 1
    h = sum(sub[:, r:r + n_cmp, r] for r in range(CMP_RATIO))
    pos_bias = jnp.einsum('cpd,cpde->ce', cmp_pos, cmp_w1.reshape(2, BLOCK_CMP, HEAD_DIM, CMP_HIDDEN))
    h = jax.nn.gelu(h + pos_bias[:, None, :])
    out = jnp.einsum('bncge,ced->bncgd', h, cmp_w2)
    return rmsnorm(out[:, :, 0], k_norm_g[0]), out[:, :, 1]

def overlap_matrix(n_cmp, n_sel):
    cs = jnp.arange(n_cmp)[:, None] * STRIDE_CMP
    js = jnp.arange(n_sel)[None, :] * SEL_BLOCK
    return ((cs < js + SEL_BLOCK) & (cs + BLOCK_CMP > js)).astype(jnp.float32)

def alibi_attend(q, pos_q, k, v, kpos, slopes, max_dist=None):
    s = jnp.einsum('btgjd,bsgd->bgjts', q, k).astype(jnp.float32) * SCALE
    dist = (pos_q[:, None] - kpos[None, :]).astype(jnp.float32)
    mask = (dist >= 0) & (kpos >= 0)[None, :]
    if max_dist is not None:
        mask = mask & (dist <= max_dist)
    s = s - slopes[:, :, None, None] * dist
    p = masked_softmax(s, mask)
    o = jnp.einsum('bgjts,bsgd->btgjd', p.astype(v.dtype), v)
    return o, p

def cmp_and_select(q, pos_q, kc, vc, overlap, slopes):
    n_cmp, n_sel = overlap.shape
    kpos = jnp.arange(n_cmp) * STRIDE_CMP + (BLOCK_CMP - 1)
    o, p = alibi_attend(q, pos_q, kc, vc, kpos, slopes)
    imp = jnp.einsum('bgjtn,nk->btgk', p, overlap)
    blk = jnp.arange(n_sel)[None, :]
    cur = (pos_q // SEL_BLOCK)[:, None]
    forced = (blk == 0) | (blk == cur) | (blk == cur - 1)
    valid = blk * SEL_BLOCK <= pos_q[:, None]
    score = jnp.where(valid[None, :, None, :],
                      imp + jnp.where(forced, FORCE_BONUS, 0.0)[None, :, None, :], NEG_INF)
    _, idx = lax.top_k(score, min(TOP_BLOCKS, n_sel))
    return o, idx

def sel_attend(q, pos_q, kb, vb, idx, slopes):
    s = jnp.einsum('btgjd,btgnrd->btgjnr', q, kb).astype(jnp.float32) * SCALE
    kpos = idx[..., None] * SEL_BLOCK + jnp.arange(SEL_BLOCK)
    dist = (pos_q[None, :, None, None, None] - kpos).astype(jnp.float32)
    s = s - slopes[None, None, :, :, None, None] * dist[:, :, :, None]
    p = masked_softmax(s, (dist >= 0)[:, :, :, None], axis=(-2, -1))
    return jnp.einsum('btgjnr,btgnrd->btgjd', p.astype(vb.dtype), vb)

def combine_branches(gates, o_cmp, o_sel, o_win):
    g = gates[..., None]
    o = g[:, :, 0] * o_cmp + g[:, :, 1] * o_sel + g[:, :, 2] * o_win
    return o.astype(o_cmp.dtype)

def nsa_prompt(q, gates, cmp_rows, sel_rows, win_rows, k_norm_g, cmp_pos, cmp_w1, cmp_w2, slopes):
    B, T = q.shape[:2]
    kc, vc = compress(sub_proj(cmp_rows, cmp_w1), k_norm_g, cmp_pos, cmp_w1, cmp_w2)
    n_sel = -(-T // SEL_BLOCK)
    overlap = overlap_matrix(kc.shape[1], n_sel)
    sel_blocks = jnp.pad(sel_rows, ((0, 0), (0, n_sel * SEL_BLOCK - T), (0, 0), (0, 0), (0, 0))
                         ).reshape(B, n_sel, SEL_BLOCK, 2, KV_HEADS, HEAD_DIM)
    win_pad = jnp.pad(win_rows, ((0, 0), (WINDOW, 0), (0, 0), (0, 0), (0, 0)))
    span = WINDOW + Q_BLOCK
    n_qb = T // Q_BLOCK
    bi = jnp.arange(B)[:, None, None, None]
    gi = jnp.arange(KV_HEADS)[None, None, :, None]

    def query_block(args):
        i, qb, gb = args
        pb = i * Q_BLOCK + jnp.arange(Q_BLOCK)
        o_cmp, idx = cmp_and_select(qb, pb, kc, vc, overlap, slopes)
        blk = sel_blocks[bi, idx, :, :, gi]
        o_sel = sel_attend(qb, pb, blk[..., 0, :], blk[..., 1, :], idx, slopes)
        kw = lax.dynamic_slice_in_dim(win_pad, i * Q_BLOCK, span, axis=1)
        kpos = i * Q_BLOCK - WINDOW + jnp.arange(span)
        o_win, _ = alibi_attend(qb, pb, kw[:, :, 0], kw[:, :, 1], kpos, slopes, WINDOW)
        return combine_branches(gb, o_cmp, o_sel, o_win)

    qs = jnp.moveaxis(q.reshape(B, n_qb, Q_BLOCK, KV_HEADS, GROUP, HEAD_DIM), 1, 0)
    gs = jnp.moveaxis(gates.reshape(B, n_qb, Q_BLOCK, N_BRANCH, KV_HEADS, GROUP), 1, 0)
    o = lax.map(query_block, (jnp.arange(n_qb), qs, gs))
    o = jnp.moveaxis(o, 0, 1).reshape(B, T, KV_HEADS, GROUP, HEAD_DIM)
    return o, win_rows[:, -min(WINDOW, T):]

def nsa_sample(q, gates, cmp_rows, sel_rows, win_rows, cache_cmp, cache_sel, cache_win_l, page_table,
               layer, k_norm_g, cmp_pos, cmp_w1, cmp_w2, slopes):
    DB, DS = q.shape[:2]
    n_pages = page_table.shape[1]
    past_len = n_pages * PAGE_SIZE
    pos_q = past_len + jnp.arange(DS)
    past_cmp = cache_cmp[layer, page_table].reshape(DB, past_len, 2, KV_HEADS, HEAD_DIM)
    sub = jnp.concatenate([sub_proj(past_cmp, cmp_w1), sub_proj(cmp_rows, cmp_w1)], axis=1)
    kc, vc = compress(sub, k_norm_g, cmp_pos, cmp_w1, cmp_w2)
    n_sel = -(-(past_len + DS) // SEL_BLOCK)
    overlap = overlap_matrix(kc.shape[1], n_sel)
    o_cmp, idx = cmp_and_select(q, pos_q, kc, vc, overlap, slopes)
    n_past_blk = past_len // SEL_BLOCK
    blk_per_page = PAGE_SIZE // SEL_BLOCK
    n_tail = n_sel - n_past_blk
    bi = jnp.arange(DB)[:, None, None, None]
    gi = jnp.arange(KV_HEADS)[None, None, :, None]
    jp = jnp.minimum(idx, n_past_blk - 1)
    phys = page_table[bi, jp // blk_per_page]
    rows = (jp % blk_per_page)[..., None] * SEL_BLOCK + jnp.arange(SEL_BLOCK)
    from_past = cache_sel[layer, phys[..., None], rows, :, gi[..., None]]
    tail = jnp.pad(sel_rows, ((0, 0), (0, n_tail * SEL_BLOCK - DS), (0, 0), (0, 0), (0, 0))
                   ).reshape(DB, n_tail, SEL_BLOCK, 2, KV_HEADS, HEAD_DIM)
    jt = jnp.clip(idx - n_past_blk, 0, n_tail - 1)
    from_new = tail[bi, jt, :, :, gi]
    blk = jnp.where((idx >= n_past_blk)[..., None, None, None], from_new, from_past)
    o_sel = sel_attend(q, pos_q, blk[..., 0, :], blk[..., 1, :], idx, slopes)
    ext = jnp.concatenate([cache_win_l, win_rows], axis=1)
    kpos = past_len - cache_win_l.shape[1] + jnp.arange(ext.shape[1])
    o_win, _ = alibi_attend(q, pos_q, ext[:, :, 0], ext[:, :, 1], kpos, slopes, WINDOW)
    o = combine_branches(gates, o_cmp, o_sel, o_win)
    return o, ext[:, -min(WINDOW, ext.shape[1]):]

def pool_mix(u, prev, pos0, pool_w, pool_scale):
    B, T, _ = u.shape
    ext = jnp.concatenate([prev, u], axis=1)
    ef = ext.astype(jnp.float32)
    cs = jnp.concatenate([jnp.zeros((B, 1, POOL_WIDTH), jnp.float32), jnp.cumsum(ef, axis=1)], axis=1)
    pos = pos0 + jnp.arange(T)
    cur = ef[:, POOL_STATE:]
    end = cs[:, POOL_STATE + 1:]
    diffs = []
    for g, w in enumerate(POOL_WINDOWS):
        c = slice(g * POOL_GROUP_WIDTH, (g + 1) * POOL_GROUP_WIDTH)
        start = cs[:, POOL_STATE + 1 - w:POOL_STATE + 1 - w + T, c]
        count = jnp.minimum(pos + 1, w).astype(jnp.float32)[None, :, None]
        diffs.append((end[..., c] - start) / count - cur[..., c])
    d = jnp.stack(diffs, axis=2)
    y = jnp.einsum('btgc,gce->btge', d, pool_w.astype(jnp.float32)).reshape(B, T, POOL_WIDTH)
    y = y * pool_scale.astype(jnp.float32)
    return y.astype(u.dtype), ext[:, -POOL_STATE:]

def peer_ffn(h, peer_wq, peer_subkeys, expert_u, expert_v):
    B, T, D = h.shape
    n = B * T
    xf = jnp.pad(h.reshape(n, D), ((0, (-n) % PEER_BLOCK), (0, 0)))

    def block(xt):
        q = jnp.einsum('td,dc->tc', xt, peer_wq).reshape(PEER_BLOCK, PEER_HEADS, 2, D_KEY // 2)
        s = jnp.einsum('thcd,hckd->thck', q, peer_subkeys).astype(jnp.float32)
        sv, si = lax.top_k(s, PEER_TOPK)
        cand = (sv[:, :, 0, :, None] + sv[:, :, 1, None, :]).reshape(PEER_BLOCK, PEER_HEADS, PEER_TOPK * PEER_TOPK)
        cv, ci = lax.top_k(cand, PEER_TOPK)
        i1 = jnp.take_along_axis(si[:, :, 0], ci // PEER_TOPK, axis=-1)
        i2 = jnp.take_along_axis(si[:, :, 1], ci % PEER_TOPK, axis=-1)
        expert = i1 * N_KEYS + i2
        gate = jax.nn.softmax(cv, axis=-1)
        a = jax.nn.gelu(jnp.einsum('td,thkd->thk', xt, expert_u[expert]).astype(jnp.float32))
        return jnp.einsum('thk,thkd->td', (gate * a).astype(xt.dtype), expert_v[expert])

    out = lax.map(block, xf.reshape(-1, PEER_BLOCK, D))
    return out.reshape(-1, D)[:n].reshape(B, T, D)

def finish(x, o_attn, y_pool, w_out, norm2_g, peer_wq, peer_subkeys, expert_u, expert_v):
    B, T, _ = x.shape
    mix = jnp.concatenate([o_attn.reshape(B, T, ATTN_WIDTH), y_pool], axis=-1)
    h = x + jnp.einsum('btc,cd->btd', mix, w_out)
    return h + peer_ffn(rmsnorm(h, norm2_g), peer_wq, peer_subkeys, expert_u, expert_v)

def setup_inputs(seed: int = 0) -> dict:
    key = jax.random.key(seed)
    ks = jax.random.split(key, 24)
    n_pages = PAST_LEN // PAGE_SIZE
    n_phys = (5 * DEC_BATCH * n_pages + 3) // 4
    w_buf = min(WINDOW, PAST_LEN)

    def nrm(k, shape, scale):
        return scale * jax.random.normal(k, shape, jnp.float32)

    page_table = jax.random.permutation(ks[6], n_phys)[:DEC_BATCH * n_pages].reshape(
        DEC_BATCH, n_pages).astype(jnp.int32)
    return {
        'x_prompt': nrm(ks[0], (BATCH, SEQ, D_MODEL), 1.0),
        'x_sample': nrm(ks[1], (DEC_BATCH, DEC_SEQ, D_MODEL), 1.0),
        'cache_cmp': nrm(ks[2], (DEPTH, n_phys, PAGE_SIZE, 2, KV_HEADS, HEAD_DIM), 1.0),
        'cache_sel': nrm(ks[3], (DEPTH, n_phys, PAGE_SIZE, 2, KV_HEADS, HEAD_DIM), 1.0),
        'cache_win': nrm(ks[4], (DEPTH, DEC_BATCH, w_buf, 2, KV_HEADS, HEAD_DIM), 1.0),
        'state_pool': nrm(ks[5], (DEPTH, DEC_BATCH, POOL_STATE, POOL_WIDTH), 1.0),
        'page_table': page_table,
        'norm1_g': 1.0 + nrm(ks[7], (DEPTH, D_MODEL), 0.02),
        'w_in': nrm(ks[8], (DEPTH, D_MODEL, IN_COLS), D_MODEL ** -0.5),
        'q_norm_g': 1.0 + nrm(ks[9], (DEPTH, HEAD_DIM), 0.02),
        'k_norm_g': 1.0 + nrm(ks[10], (DEPTH, N_BRANCH, HEAD_DIM), 0.02),
        'cmp_pos': nrm(ks[11], (DEPTH, 2, BLOCK_CMP, HEAD_DIM), 0.02),
        'cmp_w1': nrm(ks[12], (DEPTH, 2, BLOCK_CMP * HEAD_DIM, CMP_HIDDEN), (BLOCK_CMP * HEAD_DIM) ** -0.5),
        'cmp_w2': nrm(ks[13], (DEPTH, 2, CMP_HIDDEN, HEAD_DIM), CMP_HIDDEN ** -0.5),
        'pool_w': nrm(ks[14], (DEPTH, POOL_GROUPS, POOL_GROUP_WIDTH, POOL_GROUP_WIDTH), POOL_GROUP_WIDTH ** -0.5),
        'pool_scale': 1.0 + nrm(ks[15], (DEPTH, POOL_WIDTH), 0.1),
        'w_out': nrm(ks[16], (DEPTH, MIX_WIDTH, D_MODEL), MIX_WIDTH ** -0.5),
        'norm2_g': 1.0 + nrm(ks[17], (DEPTH, D_MODEL), 0.02),
        'peer_wq': nrm(ks[18], (DEPTH, D_MODEL, PEER_HEADS * D_KEY), D_MODEL ** -0.5),
        'peer_subkeys': nrm(ks[19], (DEPTH, PEER_HEADS, 2, N_KEYS, D_KEY // 2), (D_KEY // 2) ** -0.5),
        'expert_u': nrm(ks[20], (DEPTH, N_EXPERTS, D_MODEL), D_MODEL ** -0.5),
        'expert_v': nrm(ks[21], (DEPTH, N_EXPERTS, D_MODEL), 0.5),
    }

def reference(x_prompt, x_sample, cache_cmp, cache_sel, cache_win, state_pool, page_table,
              norm1_g, w_in, q_norm_g, k_norm_g, cmp_pos, cmp_w1, cmp_w2, pool_w, pool_scale,
              w_out, norm2_g, peer_wq, peer_subkeys, expert_u, expert_v):
    slopes = alibi_slopes()
    B = x_prompt.shape[0]
    past_len = page_table.shape[1] * PAGE_SIZE
    xp, xs = x_prompt, x_sample
    cmp_p, cmp_s, sel_p, sel_s, win_p, win_s, pool_p, pool_s = [], [], [], [], [], [], [], []
    for l in range(DEPTH):
        q, g, cmp_r, sel_r, win_r, u = project(xp, norm1_g[l], w_in[l], q_norm_g[l], k_norm_g[l])
        o, win_state = nsa_prompt(q, g, cmp_r, sel_r, win_r, k_norm_g[l], cmp_pos[l], cmp_w1[l], cmp_w2[l], slopes)
        y_pool, pool_state = pool_mix(u, jnp.zeros((B, POOL_STATE, POOL_WIDTH), u.dtype), 0, pool_w[l], pool_scale[l])
        xp = finish(xp, o, y_pool, w_out[l], norm2_g[l], peer_wq[l], peer_subkeys[l], expert_u[l], expert_v[l])
        cmp_p.append(cmp_r)
        sel_p.append(sel_r)
        win_p.append(win_state)
        pool_p.append(pool_state)
        q, g, cmp_r, sel_r, win_r, u = project(xs, norm1_g[l], w_in[l], q_norm_g[l], k_norm_g[l])
        o, win_state = nsa_sample(q, g, cmp_r, sel_r, win_r, cache_cmp, cache_sel, cache_win[l], page_table, l,
                                  k_norm_g[l], cmp_pos[l], cmp_w1[l], cmp_w2[l], slopes)
        y_pool, pool_state = pool_mix(u, state_pool[l], past_len, pool_w[l], pool_scale[l])
        xs = finish(xs, o, y_pool, w_out[l], norm2_g[l], peer_wq[l], peer_subkeys[l], expert_u[l], expert_v[l])
        cmp_s.append(cmp_r)
        sel_s.append(sel_r)
        win_s.append(win_state)
        pool_s.append(pool_state)
    y_prompt = xp
    y_sample = xs
    cmp_rows_prompt = jnp.stack(cmp_p)
    cmp_rows_sample = jnp.stack(cmp_s)
    sel_rows_prompt = jnp.stack(sel_p)
    sel_rows_sample = jnp.stack(sel_s)
    win_prompt = jnp.stack(win_p)
    win_sample = jnp.stack(win_s)
    pool_prompt = jnp.stack(pool_p)
    pool_sample = jnp.stack(pool_s)
    return (y_prompt, y_sample, cmp_rows_prompt, cmp_rows_sample, sel_rows_prompt, sel_rows_sample,
            win_prompt, win_sample, pool_prompt, pool_sample)


_drawn_inputs = setup_inputs


def setup_inputs(seed=0):
    import zlib

    import numpy as np

    out = dict(_drawn_inputs(seed))
    spreads = {}
    factors = {'q_norm_g': 4.805, 'k_norm_g': 3.841, 'cmp_pos': 3.782}
    for name, (base, spread) in spreads.items():
        noise = np.random.default_rng([zlib.crc32(name.encode()), seed]).standard_normal(out[name].shape)
        drawn = base * np.exp(spread * noise) if base else spread * noise
        out[name] = jnp.asarray(drawn.astype(out[name].dtype))
    for name, factor in factors.items():
        out[name] = (out[name] * factor).astype(out[name].dtype)
    return out
```

```python
import numpy as np
from contextlib import ExitStack

import concourse.bass as bass
from concourse import mybir

F32 = mybir.dt.float32
F32R = mybir.dt.float32r
BF16 = mybir.dt.bfloat16
I32 = mybir.dt.int32
U32 = mybir.dt.uint32
ALU = mybir.AluOpType
ACT = mybir.ActivationFunctionType
AX = mybir.AxisListType

P = 128
D = 1024
KC = D // P
SEQ, DB, DS = 512, 8, 4
ST = DB * DS
T = SEQ + ST
HALF = T // 2
HD, KVH, GRP = 64, 2, 4
NH = KVH * GRP
PAST, PAGE, NPAGE, NPHYS = 1024, 128, 8, 80
WIN = 512
QT = SEQ // P
NTT = 5
ZT_Q, ZT_KV, ZT_U, NZT = 0, 4, 10, 14
STRIDE = 16
NSUB_P, NSUB_S = SEQ // STRIDE, PAST // STRIDE
NCMP_P, NCMP_S = NSUB_P - 1, NSUB_S - 1
SELB, NBLK = 64, 16
POOLW = (2, 4, 8, 16)
PST = 15
PH, NKEY, TOPK = 8, 128, 16
NEG = -1e30
EPS = 1e-6
ROWS = 128
BPT = 4


GE = 8
NG = NKEY // GE


def constants():
    p = np.arange(P)
    slope = 2.0 ** -np.arange(1, NH + 1).reshape(KVH, GRP)
    c = {}
    c["c_ident"] = np.eye(P)
    c["c_mean_d"] = np.full((P, P), 1.0 / D)
    c["c_mean_head"] = (p[:, None] // HD == p[None, :] // HD) / HD
    dist = p[:, None] + 384 - np.arange(512)[None, :]
    c["c_causal"] = np.where(dist >= 0, -dist, NEG)
    t = np.arange(QT)[None, :, None] * P + p[:, None, None]
    dist = t - (np.arange(NCMP_P)[None, None, :] * STRIDE + 31)
    c["c_cmp_p"] = np.where(dist >= 0, -dist, NEG).reshape(P, QT * NCMP_P)
    c["c_row_valid"] = (t[:, :, 0] >= 31)
    c["c_qscale"] = np.repeat(HD ** -0.5 / slope, HD, axis=0)
    c["c_slope"] = np.broadcast_to(slope.T.reshape(1, NH), (P, NH))
    r = np.arange(ROWS)
    rb, rg, rj, rt = r // 32, r // 16 % 2, r // 4 % 4, r % 4
    c["c_sel_s"] = -(PAST + rt[:, None] - np.arange(PAST)[None, :])
    dist = WIN + rt[:, None] - np.arange(WIN)[None, :]
    c["c_win_s"] = np.where(dist <= WIN, -dist, NEG)
    c["c_cmp_s"] = -(PAST + rt[:, None] - (np.arange(NCMP_S)[None, :] * STRIDE + 31))
    k = np.arange(ST)
    tail = []
    for bt in range(2):
        ok = (k[None, :] // DS == (bt * BPT + rb)[:, None]) & (k[None, :] % DS <= rt[:, None])
        tail.append(np.where(ok, -(rt[:, None] - k[None, :] % DS), NEG))
    c["c_tail_s"] = np.concatenate(tail, 1)
    c["c_slope_s"] = slope[rg, rj][:, None]
    c["c_same_bgt"] = (rb[:, None] == rb) & (rg[:, None] == rg) & (rt[:, None] == rt)
    tok = np.zeros((P, 2 * ROWS))
    for bt in range(2):
        tok[(bt * BPT + rb) * DS + rt, bt * ROWS + r] = 1
    c["c_tok_row"] = tok
    gj = np.arange(NH)
    c["c_gate_row"] = np.tile((gj[None, :] == (rg * GRP + rj)[:, None]), (1, 3))
    c["c_blk"] = np.broadcast_to(np.arange(NBLK)[None, :], (P, NBLK))
    cnt = np.stack([w / np.minimum(np.arange(16) + 1, w) for w in POOLW])
    c["c_pool_fix"] = np.broadcast_to(cnt.reshape(1, 64), (P, 64))
    c["c_eps"] = np.full((P, 1), EPS)
    c["c_iota"] = np.broadcast_to(np.arange(P)[None, :], (P, P))
    return {k: np.ascontiguousarray(v, dtype=np.float32) for k, v in c.items()}


def bank(g, k, n=1):
    return g.ps[:, 512 * k:512 * (k + n)]


class Shared:
    pass


def halves(x):
    return x.rearrange("p (h n) -> p h n", h=2)


def memory(nc, ctx):
    sb = lambda n, s, d=F32: ctx.enter_context(nc.sbuf_tensor("sb_" + n, s, d))
    sem = lambda n: ctx.enter_context(nc.semaphore(n))
    return sb, sem


def project(nc, g):
    with ExitStack() as ctx:
        sb, sem = memory(nc, ctx)
        sq = sb("sq", [P, 2, T])
        rstd = sb("rstd", [P, 2, T])
        xn = sb("xn", [P, KC, T])
        w = [sb(f"w_tile{k}", [P, KC * P]) for k in range(2)]
        wg = sb("w_gates", [P, KC, 24])
        norm1 = sb("norm1", [P, KC])
        hg = sb("head_gains", [P, 4])
        gq = sb("gq", [P, GRP])
        x_in, consts_in = sem("x_in"), sem("consts_in")
        w_in = [sem("w_in0"), sem("w_in1")]
        sq_ready, sq_used, std_ready, rstd_ready, xn_ready = map(sem, ("sq_ready", "sq_used", "std_ready", "rstd_ready", "xn_ready"))
        hstd_ready = sem("hstd_ready")
        z_ready = sem("z_ready")
        z_act, z_dve = sem("z_act"), sem("z_dve")
        gates_mm, hsq_ready, hms_ready, hrstd_ready, hn_ready, gq_ready = map(
            sem, ("gates_mm", "hsq_ready", "hms_ready", "hrstd_ready", "hn_ready", "gq_ready"))
        kept, stored = sem("kept"), sem("stored")
        NORMED = [0, 1, 2, 3, 6, 8]
        n_const = 16 * (len(g.c) + 3)
        block = ctx.enter_context(nc.Block())

        @block.sync
        def _(sp):
            sp.dma_start(g.xT[:, 0:4, :], g.a["xT"][:, 0:4, :]).then_inc(x_in, 16)
            sp.dma_start(g.xT[:, 4:8, :], g.a["xT"][:, 4:8, :]).then_inc(x_in, 16)
            for n in g.c:
                sp.dma_start(g.c[n][:, :], g.a[n]).then_inc(consts_in, 16)
            sp.dma_start(norm1[:, :], g.a["norm1"]).then_inc(consts_in, 16)
            sp.dma_start(hg[:, :], g.a["head_gains"]).then_inc(consts_in, 16)
            sp.dma_start(wg[:, :, :], g.a["w_gate"]).then_inc(consts_in, 16)
            sp.wait_ge(hn_ready, len(NORMED))
            sp.dma_start(g.a["out_kv"], g.zT[:, ZT_KV:ZT_U, :]).then_inc(stored, 16)
            sp.dma_start(g.a["out_u"], g.zT[:, ZT_U:NZT, SEQ - PST:T]).then_inc(stored, 16)
            sp.wait_ge(stored, 32)
            sp.wait_ge(kept, 32)

        @block.gpsimd
        def _(pool):
            for i in range(NZT):
                if i >= 2:
                    pool.wait_ge(z_ready, i - 1)
                pool.dma_start(w[i % 2][:, :], g.a["w_in"][i]).then_inc(w_in[i % 2], 16)
            pool.dma_start(g.a["out_win_past"], g.a["cache_win_kept"]).then_inc(kept, 16)
            pool.dma_start(g.a["out_pool_past"], g.a["state_pool_kept"]).then_inc(kept, 16)

        @block.scalar
        def _(act):
            def head_std(n):
                act.wait_ge(hms_ready, n + 1)
                if n >= 2:
                    act.wait_ge(hn_ready, n - 1)
                nc.scalar.activation(halves(rstd[:, n % 2]), halves(bank(g, 2 * (n % 2), 2))[:, :, 0:HALF], ACT.Sqrt,
                                     bias=g.c["c_eps"][:, :]).then_inc(hstd_ready, 1)

            act.wait_ge(consts_in, n_const)
            act.wait_ge(x_in, 32)
            for k in range(KC):
                if k >= 2:
                    act.wait_ge(sq_used, k - 1)
                nc.scalar.activation(sq[:, k % 2], g.xT[:, k], ACT.Square).then_inc(sq_ready, 1)
            act.wait_ge(sq_used, KC)
            nc.scalar.activation(halves(rstd[:, 0]), halves(bank(g, 0, 2))[:, :, 0:HALF], ACT.Sqrt, bias=g.c["c_eps"][:, :]).then_inc(std_ready, 1)
            act.sem_inc(z_act, 2)
            with act.Fori(0, NZT // 2) as i:
                for par in range(2):
                    act.wait_ge(z_ready, 2 * i + (par + 1))
                    nc.scalar.activation(g.zT[:, bass.ds(2 * i + par, 1), 0:HALF], bank(g, 2 * par)[:, None, 0:HALF],
                                         ACT.Copy).then_inc(z_act, 1)
            act.wait_ge(z_dve, NZT + 2)
            act.wait_ge(z_act, NZT + 2)
            for n, tile in enumerate(NORMED):
                if n >= 2:
                    act.wait_ge(hms_ready, n - 1)
                nc.scalar.activation(sq[:, n % 2], g.zT[:, tile], ACT.Square).then_inc(hsq_ready, 1)
                if n:
                    head_std(n - 1)
            head_std(len(NORMED) - 1)
            act.wait_ge(gates_mm, 1)
            for tt in range(NTT):
                r = min(P, T - tt * P)
                nc.scalar.activation(g.gates[0:r, tt], bank(g, 4)[0:r, 24 * tt:24 * tt + 24], ACT.Sigmoid)

        @block.tensor
        def _(pe):
            pe.wait_ge(consts_in, n_const)
            for k in range(KC):
                pe.wait_ge(sq_ready, k + 1)
                for h in range(2):
                    last = nc.tensor.matmul(bank(g, h)[:, 0:HALF], g.c["c_mean_d"][:, :], sq[:, k % 2, h * HALF:(h + 1) * HALF],
                                            start=(k == 0), stop=(k == KC - 1))
                last.then_inc(sq_used, 1)
            pe.wait_ge(xn_ready, KC)
            with pe.Fori(0, NZT // 2) as i:
                for par in range(2):
                    pe.wait_ge(w_in[par], 16 * i + 16)
                    pe.wait_ge(z_act, 2 * i + (par + 1))
                    pe.wait_ge(z_dve, 2 * i + (par + 1))
                    for h in range(2):
                        for k in range(KC):
                            last = nc.tensor.matmul(bank(g, 2 * par + h)[:, 0:HALF], w[par][:, k * P:(k + 1) * P],
                                                    xn[:, k, h * HALF:(h + 1) * HALF], start=(k == 0), stop=(k == KC - 1))
                    last.then_inc(z_ready, 1)
            for tt in range(NTT):
                r = min(P, T - tt * P)
                for k in range(KC):
                    last = nc.tensor.matmul(bank(g, 4)[0:r, 24 * tt:24 * tt + 24], xn[:, k, tt * P:tt * P + r], wg[:, k],
                                            start=(k == 0), stop=(k == KC - 1))
            last.then_inc(gates_mm, 1)
            pe.wait_ge(z_act, NZT + 2)
            pe.wait_ge(z_dve, NZT + 2)
            for n in range(len(NORMED)):
                pe.wait_ge(hsq_ready, n + 1)
                if n >= 2:
                    pe.wait_ge(hstd_ready, n - 1)
                for h in range(2):
                    last = nc.tensor.matmul(bank(g, 2 * (n % 2) + h)[:, 0:HALF], g.c["c_mean_head"][:, :],
                                            sq[:, n % 2, h * HALF:(h + 1) * HALF], start=True, stop=True)
                last.then_inc(hms_ready, 1)

        @block.vector
        def _(dve):
            dve.wait_ge(consts_in, n_const)
            nc.vector.tensor_scalar(gq[:, :], g.c["c_qscale"][:, :], hg[:, 0:1], None, ALU.mult).then_inc(gq_ready, 1)
            nc.vector.tensor_copy(g.kc_gain[:, :], hg[:, 1:2])
            dve.wait_ge(std_ready, 1)
            nc.vector.reciprocal(rstd[:, 0], rstd[:, 0]).then_inc(rstd_ready, 1)
            dve.wait_ge(rstd_ready, 1)
            for k in range(KC):
                nc.vector.scalar_tensor_tensor(out=xn[:, k], in0=g.xT[:, k], scalar=norm1[:, k:k + 1], in1=rstd[:, 0],
                                               op0=ALU.mult, op1=ALU.mult).then_inc(xn_ready, 1)
            dve.sem_inc(z_dve, 2)
            with dve.Fori(0, NZT // 2) as i:
                for par in range(2):
                    dve.wait_ge(z_ready, 2 * i + (par + 1))
                    nc.vector.tensor_copy(g.zT[:, bass.ds(2 * i + par, 1), HALF:T], bank(g, 2 * par + 1)[:, None, 0:HALF]).then_inc(z_dve, 1)
            dve.wait_ge(z_act, NZT + 2)
            dve.wait_ge(gq_ready, 1)
            for n, tile in enumerate(NORMED):
                dve.wait_ge(hstd_ready, n + 1)
                nc.vector.reciprocal(rstd[:, n % 2], rstd[:, n % 2]).then_inc(hrstd_ready, 1)
                dve.wait_ge(hrstd_ready, n + 1)
                gain = gq[:, tile:tile + 1] if tile < GRP else hg[:, (2 if tile == 6 else 3):(3 if tile == 6 else 4)]
                nc.vector.scalar_tensor_tensor(out=g.zT[:, tile], in0=g.zT[:, tile], scalar=gain, in1=rstd[:, n % 2],
                                               op0=ALU.mult, op1=ALU.mult).then_inc(hn_ready, 1)


def compress(nc, g):
    with ExitStack() as ctx:
        sb, sem = memory(nc, ctx)
        CH = KVH * 2
        EB = 4
        w1 = sb("w1", [P, 2, 2, 8, P])
        w2 = sb("w2", [P, 2, HD])
        pos = sb("pos", [P, 2, 2, 8])
        bias = sb("pos_bias", [P, 2])
        tmp = sb("cmp_rows", [P, 2, 2, 8, NSUB_P])
        cmpP = sb("cmp_prompt", [P, 2, 2, 8 * NSUB_P])
        cmpS = sb("cmp_pages", [P, EB, NPAGE, 2, 2, 8, 8])
        h0 = sb("h0", [P, 2, 256])
        hS = sb("h_sample", [P, 2, 2, EB, NCMP_S])
        hP = sb("h_prompt", [P, 2, 2, NCMP_P])
        sqk = sb("sqk", [P, 256])
        rk = sb("rk", [P, 256])
        w_in, table_in, page_in, rows_in, tmp_ready = map(sem, ("cw_in", "table_in", "page_in", "rows_in", "tmp_ready"))
        bias_mm, bias_ready, sub_mm, a_ready, sum_ready, h_ready = map(sem, ("bias_mm", "bias_ready", "sub_mm", "a_ready", "sum_ready", "h_ready"))
        kv_mm, ksq, kms, kstd, krs, kn, v_out = map(sem, ("kv_mm", "ksq", "kms", "kstd", "krs", "kn", "v_out"))
        tr_mm, tr_out = sem("tr_mm"), sem("tr_out")
        block = ctx.enter_context(nc.Block())
        units = [("P", 0, 0), ("P", 1, 0)] + [(b, c, gg) for b in range(2) for c in range(2) for gg in range(2)]
        NU = len(units)

        @block.sync
        def _(sp):
            sp.dma_start(g.table[:, :], g.a["page_table"]).then_inc(table_in, 16)
            sp.dma_start(w1[:, :, :, :, :].rearrange("p c r s e -> p (c r s e)"), g.a["cmp_w1"]).then_inc(w_in, 16)
            sp.dma_start(w2[:, :, :].rearrange("p c d -> p (c d)"), g.a["cmp_w2"]).then_inc(w_in, 16)
            sp.dma_start(pos[:, :, :, :].rearrange("p c r s -> p (c r s)"), g.a["cmp_pos"]).then_inc(w_in, 16)
            sp.wait_ge(tmp_ready, 2)
            for gg in range(2):
                for s2 in range(2):
                    sp.dma_start(cmpP[s2 * HD:(s2 + 1) * HD, :, gg, :],
                                 tmp[gg * HD:(gg + 1) * HD, :, s2].rearrange("p c s n -> p c (s n)")).then_inc(rows_in, 16)

        @block.gpsimd
        def _(pool):
            pool.wait_ge(table_in, 16)
            for half in range(2):
                if half:
                    pool.wait_ge(sub_mm, 6)
                for k in range(EB * NPAGE):
                    page = pool.value_load(g.table[0:1, half * EB * NPAGE + k:half * EB * NPAGE + k + 1], min_val=0, max_val=NPHYS - 1)
                    pool.dma_start(cmpS[:, k // NPAGE, k % NPAGE].rearrange("p c g s n -> p (c g s n)"),
                                   g.a["cache_cmp"][bass.ds(page, 1)].rearrange("a p n -> p (a n)")).then_inc(page_in, 16)

        @block.tensor
        def _(pe):
            pe.wait_ge(w_in, 48)
            for c in range(2):
                for n in range(16):
                    last = nc.tensor.matmul(bank(g, 7)[:, c:c + 1], w1[:, c, n // 8, n % 8], pos[:, c, n // 8, n % 8:n % 8 + 1],
                                            start=(n == 0), stop=(n == 15))
            last.then_inc(bias_mm, 1)
            for n, tile in enumerate((7, 9)):
                for tt in range(NTT):
                    r = min(P, T - tt * P)
                    at = bank(g, 5 + n) if tt < 4 else bank(g, 4)[:, n * P:(n + 1) * P]
                    off = (tt % 4) * P
                    last = nc.tensor.transpose(at[0:r, off:off + P] if tt < 4 else at[0:r, :], g.zT[:, tile, tt * P:tt * P + r], g.c["c_ident"][:, :])
            last.then_inc(tr_mm, 1)
            for u, (part, c, gg) in enumerate(units):
                if part == "P":
                    pe.wait_ge(rows_in, 64)
                else:
                    pe.wait_ge(page_in, 16 * EB * NPAGE * (part + 1))
                if u >= 2:
                    pe.wait_ge(sum_ready, u - 1)
                for r in range(2):
                    out = bank(g, 2 * (u % 2) + r)
                    for s in range(8):
                        if part == "P":
                            mov, n = cmpP[:, c, :, s * NSUB_P:(s + 1) * NSUB_P], 64
                        else:
                            mov, n = cmpS[:, :, :, c, gg, s].rearrange("p b q n -> p (b q) n"), 256
                        last = nc.tensor.matmul(out[:, 0:n], w1[:, c, r, s], mov, start=(s == 0), stop=(s == 7))
                last.then_inc(sub_mm, 1)
                if part == "P" and c == 1 or part != "P" and (c, gg) == (1, 1):
                    e = 0 if part == "P" else 1 + part
                    pe.wait_ge(h_ready, u + 1)
                    pe.wait_ge(tr_out, 2)
                    if e:
                        pe.wait_ge(kn, e)
                        pe.wait_ge(v_out, e)
                    if part == "P":
                        for k in range(2):
                            nc.tensor.matmul(bank(g, 4)[k * HD:(k + 1) * HD, 0:NCMP_P], w2[:, 0], hP[:, 0, k], start=True, stop=True)
                        for k in range(2):
                            last = nc.tensor.matmul(bank(g, 5)[0:NCMP_P, k * HD:(k + 1) * HD], hP[:, 1, k], w2[:, 1], start=True, stop=True)
                    else:
                        for k in range(2):
                            nc.tensor.matmul(bank(g, 4)[k * HD:(k + 1) * HD, 0:EB * NCMP_S], w2[:, 0], hS[:, 0, k].rearrange("p b n -> p (b n)"), start=True, stop=True)
                        for b in range(EB):
                            for k in range(2):
                                last = nc.tensor.matmul(bank(g, 5)[0:NCMP_S, b * P + k * HD:b * P + (k + 1) * HD], hS[:, 1, k, b], w2[:, 1], start=True, stop=True)
                    last.then_inc(kv_mm, 1)
                    n = NCMP_P if part == "P" else EB * NCMP_S
                    pe.wait_ge(ksq, e + 1)
                    nc.tensor.matmul(bank(g, 6)[:, 0:n], g.c["c_mean_head"][:, :], sqk[:, 0:n], start=True, stop=True).then_inc(kms, 1)

        @block.scalar
        def _(act):
            act.wait_ge(bias_mm, 1)
            nc.scalar.activation(bias[:, :], bank(g, 7)[:, 0:2], ACT.Copy).then_inc(bias_ready, 1)
            act.wait_ge(tr_mm, 1)
            nc.scalar.activation(g.v_sel[:, 0:4], bank(g, 5).rearrange("p (t n) -> p t n", t=4), ACT.Copy).then_inc(tr_out, 1)
            act.wait_ge(bias_ready, 1)
            for u, (part, c, gg) in enumerate(units):
                n = 64 if part == "P" else 256
                act.wait_ge(sub_mm, u + 1)
                if u >= 2:
                    act.wait_ge(h_ready, u - 1)
                nc.scalar.activation(h0[:, u % 2, 0:n], bank(g, 2 * (u % 2))[:, 0:n], ACT.Identity, bias=bias[:, c:c + 1]).then_inc(a_ready, 1)
                act.wait_ge(sum_ready, u + 1)
                e = 0 if part == "P" else 1 + part
                if e == 2:
                    act.wait_ge(kv_mm, 2)
                if part == "P":
                    src = h0[:, u % 2, 0:64].rearrange("p (g n) -> p g n", g=2)[:, :, 0:NCMP_P]
                    nc.scalar.activation(hP[:, c], src, ACT.Gelu_apprx_tanh).then_inc(h_ready, 1)
                else:
                    src = h0[:, u % 2, :].rearrange("p (b n) -> p b n", b=EB)[:, :, 0:NCMP_S]
                    nc.scalar.activation(hS[:, c, gg], src, ACT.Gelu_apprx_tanh).then_inc(h_ready, 1)
                if part == "P" and c == 1 or part != "P" and (c, gg) == (1, 1):
                    n = NCMP_P if part == "P" else EB * NCMP_S
                    act.wait_ge(kv_mm, e + 1)
                    if e:
                        act.wait_ge(kms, e)
                    nc.scalar.activation(sqk[:, 0:n], bank(g, 4)[:, 0:n], ACT.Square).then_inc(ksq, 1)
                    if part == "P":
                        nc.scalar.activation(g.vc_p[0:NCMP_P, :], bank(g, 5)[0:NCMP_P, 0:P], ACT.Copy).then_inc(v_out, 1)
                    else:
                        nc.scalar.activation(g.vc_s[0:NCMP_S, EB * part:EB * part + EB], bank(g, 5)[0:NCMP_S].rearrange("p (b n) -> p b n", b=EB),
                                             ACT.Copy).then_inc(v_out, 1)
                    act.wait_ge(kms, e + 1)
                    if e:
                        act.wait_ge(kn, e)
                    nc.scalar.activation(rk[:, 0:n], bank(g, 6)[:, 0:n], ACT.Sqrt, bias=g.c["c_eps"][:, :]).then_inc(kstd, 1)

        @block.vector
        def _(dve):
            for c in range(2):
                nc.vector.tensor_copy(tmp[:, c].rearrange("p a s n -> p (a s) n"),
                                      g.zT[:, ZT_KV + c, 0:SEQ].rearrange("p (n s) -> p s n", s=STRIDE)).then_inc(tmp_ready, 1)
            dve.wait_ge(tr_mm, 1)
            nc.vector.tensor_copy(g.v_win[:, 0:4], bank(g, 6).rearrange("p (t n) -> p t n", t=4))
            nc.vector.tensor_copy(g.v_sel[0:ST, 4], bank(g, 4)[0:ST, 0:P])
            nc.vector.tensor_copy(g.v_win[0:ST, 4], bank(g, 4)[0:ST, P:2 * P]).then_inc(tr_out, 1)
            for u, (part, c, gg) in enumerate(units):
                dve.wait_ge(a_ready, u + 1)
                x = bank(g, 2 * (u % 2) + 1)
                if part == "P":
                    h = h0[:, u % 2, 0:64].rearrange("p (g n) -> p g n", g=2)[:, :, 0:NCMP_P]
                    x = x[:, 0:64].rearrange("p (g n) -> p g n", g=2)[:, :, 1:NSUB_P]
                else:
                    h = h0[:, u % 2, :].rearrange("p (b n) -> p b n", b=EB)[:, :, 0:NCMP_S]
                    x = x[:, 0:256].rearrange("p (b n) -> p b n", b=EB)[:, :, 1:NSUB_S]
                nc.vector.tensor_tensor(h, h, x, ALU.add).then_inc(sum_ready, 1)
                if part == "P" and c == 1 or part != "P" and (c, gg) == (1, 1):
                    e = 0 if part == "P" else 1 + part
                    n = NCMP_P if part == "P" else EB * NCMP_S
                    dve.wait_ge(kstd, e + 1)
                    nc.vector.reciprocal(rk[:, 0:n], rk[:, 0:n]).then_inc(krs, 1)
                    dve.wait_ge(krs, e + 1)
                    dst = g.kc_p[:, :] if part == "P" else g.kc_s[:, EB * part:EB * part + EB].rearrange("p b n -> p (b n)")
                    nc.vector.scalar_tensor_tensor(out=dst, in0=bank(g, 4)[:, 0:n], scalar=g.kc_gain[:, :], in1=rk[:, 0:n],
                                                   op0=ALU.mult, op1=ALU.mult).then_inc(kn, 1)


def pool_mixer(nc, g):
    with ExitStack() as ctx:
        sb, sem = memory(nc, ctx)
        NW = PST + SEQ
        SW_ = PST + DS
        NB = NW + DB * SW_
        ext = sb("u_ext", [P, 4, NB])
        acc = sb("u_sum", [P, 2, NB])
        diff = sb("u_diff", [P, 4, T])
        pw = sb("pool_w", [P, 4, P])
        pscale = sb("pool_scale", [P, 4])
        w_in, zero, filled, summed, scaled, fixed, diffed, pmm = map(
            sem, ("pw_in", "u_zero", "u_filled", "u_summed", "u_scaled", "u_fixed", "u_diffed", "pool_mm"))
        block = ctx.enter_context(nc.Block())
        exts = lambda a: a[:, NW:NB].rearrange("p (b n) -> p b n", b=DB)

        @block.sync
        def _(sp):
            sp.dma_start(pw[:, :, :], g.a["pool_w"]).then_inc(w_in, 16)
            sp.dma_start(pscale[:, :], g.a["pool_scale"]).then_inc(w_in, 16)
            for k in range(4):
                sp.dma_start(exts(ext[:, k])[:, :, 0:PST], g.a["state_pool_t"][:, k]).then_inc(w_in, 16)

        @block.gpsimd
        def _(pool):
            pool.memset(ext[:, :, 0:PST], 0.0)
            pool.tensor_copy(ext[:, :, PST:NW], g.zT[:, ZT_U:NZT, 0:SEQ])
            for k in range(4):
                last = pool.tensor_copy(exts(ext[:, k])[:, :, PST:SW_], g.zT[:, ZT_U + k, SEQ:T].rearrange("p (b n) -> p b n", b=DB))
            last.then_inc(filled, 1)

        @block.vector
        def _(dve):
            dve.wait_ge(w_in, 96)
            dve.wait_ge(filled, 1)
            n, m = 0, 0
            for k, wlen in enumerate(POOLW):
                src = ext[:, k]
                if k:
                    dve.wait_ge(diffed, k)
                for step in range(k + 1):
                    sh = 1 << step
                    dst = acc[:, step % 2]
                    lo = 2 * sh - 1
                    nc.vector.tensor_tensor(dst[:, lo:NW], src[:, lo:NW], src[:, lo - sh:NW - sh], ALU.add)
                    nc.vector.tensor_tensor(exts(dst)[:, :, lo:SW_], exts(src)[:, :, lo:SW_], exts(src)[:, :, lo - sh:SW_ - sh], ALU.add).then_inc(summed, 1)
                    n += 1
                    dve.wait_ge(summed, n)
                    src = dst
                nc.vector.tensor_tensor(src[:, PST:PST + 16], src[:, PST:PST + 16], g.c["c_pool_fix"][:, 16 * k:16 * k + 16], ALU.mult).then_inc(fixed, 1)
                dve.wait_ge(fixed, k + 1)
                nc.vector.scalar_tensor_tensor(out=diff[:, k, 0:SEQ], in0=src[:, PST:NW], scalar=1.0 / wlen, in1=ext[:, k, PST:NW],
                                               op0=ALU.mult, op1=ALU.subtract)
                nc.vector.scalar_tensor_tensor(out=diff[:, k, SEQ:T].rearrange("p (b n) -> p b n", b=DB), in0=exts(src)[:, :, PST:SW_],
                                               scalar=1.0 / wlen, in1=exts(ext[:, k])[:, :, PST:SW_], op0=ALU.mult, op1=ALU.subtract).then_inc(diffed, 1)

        @block.tensor
        def _(pe):
            pe.wait_ge(w_in, 96)
            for k in range(4):
                pe.wait_ge(diffed, k + 1)
                for h in range(2):
                    last = nc.tensor.matmul(bank(g, 2 * k + h)[:, 0:HALF], pw[:, k], diff[:, k, h * HALF:(h + 1) * HALF], start=True, stop=True)
                last.then_inc(pmm, 1)

        @block.scalar
        def _(act):
            act.wait_ge(w_in, 96)
            for k in range(4):
                act.wait_ge(pmm, k + 1)
                nc.scalar.activation(g.mixT[:, 4 + k].rearrange("p (h n) -> p h n", h=2),
                                     bank(g, 2 * k, 2).rearrange("p (h n) -> p h n", h=2)[:, :, 0:HALF], ACT.Copy, scale=pscale[:, k:k + 1])


def attend_prompt(nc, g):
    with ExitStack() as ctx:
        sb, sem = memory(nc, ctx)
        NU = KVH * QT
        q = sb("q_heads", [P, SEQ])
        slp = sb("slopes", [P, 2])
        nslp = sb("neg_slopes", [P, 2])
        gst = sb("gates_j", [P, QT, 6])
        ps_ = [[sb(f"p_{n}{k}", [P, w]) for n, w in (("cmp", NCMP_P), ("sel", SEQ), ("win", SEQ))] for k in range(2)]
        pt = [[sb(f"pt_{n}{k}", [P, w]) for n, w in (("cmp", P), ("sel", SEQ), ("win", SEQ))] for k in range(2)]
        mx = sb("row_max", [P, 2, 3])
        nm = sb("neg_max", [P, 2, 3])
        rs = sb("row_sum", [P, 2, 3])
        wt = sb("row_weight", [P, 2, 3])
        diag = sb("diag", [P, 2, 3, P])
        started = sem("started")
        q_ready, max_done, scores, biased, exps, diags, turned, t_act, t_dve, o_mm, o_out, c1, c2, c3 = map(sem, (
            "q_ready", "max_done", "scores", "biased", "exps", "diags", "turned", "t_act", "t_dve", "o_mm", "o_out", "c_rec", "c_wt", "c_valid"))
        block = ctx.enter_context(nc.Block())
        units = [(k // QT, k % QT) for k in range(NU)]
        KT = {1: 6, 2: 8}
        V = {1: g.v_sel, 2: g.v_win}

        def done(eng, s, j, u):
            eng.wait_ge(s, NU * j + (NU + u + 1))

        @block.vector
        def _(dve):
            dve.sem_inc(biased, NU)
            dve.sem_inc(diags, NU)
            dve.sem_inc(t_dve, NU)
            dve.sem_inc(o_out, NU)
            with dve.Fori(0, GRP) as j:
                done(dve, scores, j, -1)
                done(dve, exps, j, -1)
                nc.vector.tensor_copy(q[:, :], g.zT[:, bass.ds(j, 1), 0:SEQ].rearrange("p a n -> p (a n)"))
                nc.vector.tensor_copy(slp[:, :], g.c["c_slope"][:, bass.ds(2 * j, 2)])
                nc.vector.tensor_scalar(nslp[:, :], g.c["c_slope"][:, bass.ds(2 * j, 2)], -1.0, None, ALU.mult)
                nc.vector.tensor_copy(gst[:, :, :, None], g.gates[:, 0:QT].rearrange("p q (x j) -> p q x j", j=GRP)[:, :, :, bass.ds(j, 1)]).then_inc(q_ready, 1)
                dve.wait_ge(q_ready, j + 1)
                for s in range(NU + 2):
                    if s < NU:
                        gg, qt = units[s]
                        par = s % 2
                        n = (qt + 1) * P
                        done(dve, scores, j, s)
                        done(dve, turned, j, s - 2)
                        dve.sem_inc(started, 1)
                        nc.vector.tensor_tensor_reduce(out=ps_[par][0][:, :], in0=bank(g, 2)[:, 0:NCMP_P], in1=g.c["c_cmp_p"][:, qt * NCMP_P:(qt + 1) * NCMP_P],
                                                       scale=1.0, scalar=-3e38, op0=ALU.add, op1=ALU.max, accum_out=mx[:, par, 0:1])
                        for br in (1, 2):
                            last = nc.vector.tensor_tensor_reduce(out=ps_[par][br][:, 0:n], in0=bank(g, br - 1)[:, 0:n], in1=g.c["c_causal"][:, SEQ - n:SEQ],
                                                                  scale=1.0, scalar=-3e38, op0=ALU.add, op1=ALU.max, accum_out=mx[:, par, br:br + 1])
                        last.then_inc(max_done, 1)
                        dve.wait_ge(max_done, NU * j + (s + 1))
                        nc.vector.tensor_scalar(nm[:, par], mx[:, par], nslp[:, gg:gg + 1], None, ALU.mult).then_inc(biased, 1)
                    if 1 <= s <= NU:
                        u = s - 1
                        gg, qt = units[u]
                        par = u % 2
                        n = (qt + 1) * P
                        done(dve, exps, j, u)
                        nc.vector.reciprocal(wt[:, par], rs[:, par]).then_inc(c1, 1)
                        dve.wait_ge(c1, NU * j + (u + 1))
                        nc.vector.tensor_tensor(wt[:, par], wt[:, par], gst[:, qt].rearrange("p (b g) -> p b g", g=2)[:, :, gg], ALU.mult).then_inc(c2, 1)
                        dve.wait_ge(c2, NU * j + (u + 1))
                        nc.vector.tensor_tensor(wt[:, par, 0:1], wt[:, par, 0:1], g.c["c_row_valid"][:, qt:qt + 1], ALU.mult).then_inc(c3, 1)
                        dve.wait_ge(c3, NU * j + (u + 1))
                        for br in range(3):
                            last = nc.vector.tensor_scalar(diag[:, par, br], g.c["c_ident"][:, :], wt[:, par, br:br + 1], None, ALU.mult)
                        last.then_inc(diags, 1)
                        done(dve, turned, j, u)
                        done(dve, o_mm, j, u - 2)
                        nc.vector.tensor_copy(pt[par][2][:, 0:n], bank(g, 4)[:, 0:n]).then_inc(t_dve, 1)
                    if s >= 2:
                        u = s - 2
                        gg, qt = units[u]
                        done(dve, o_mm, j, u)
                        half = slice(gg * HD, (gg + 1) * HD)
                        nc.vector.tensor_copy(g.mixT[half, bass.ds(j, 1), qt * P:(qt + 1) * P], bank(g, 6 + u % 2)[half, None, 0:P]).then_inc(o_out, 1)

        @block.scalar
        def _(act):
            act.sem_inc(exps, NU)
            act.sem_inc(t_act, NU)
            with act.Fori(0, GRP) as j:
                for s in range(NU + 1):
                    if s < NU:
                        gg, qt = units[s]
                        par = s % 2
                        n = (qt + 1) * P
                        done(act, biased, j, s)
                        for br, m in ((0, NCMP_P), (1, n), (2, n)):
                            last = nc.scalar.activation(ps_[par][br][:, 0:m], ps_[par][br][:, 0:m], ACT.Exp, bias=nm[:, par, br:br + 1],
                                                        scale=slp[:, gg:gg + 1], accum_out=rs[:, par, br:br + 1])
                        last.then_inc(exps, 1)
                    if s >= 1:
                        u = s - 1
                        gg, qt = units[u]
                        par = u % 2
                        n = (qt + 1) * P
                        done(act, turned, j, u)
                        done(act, o_mm, j, u - 2)
                        nc.scalar.activation(pt[par][0][0:NCMP_P, :], bank(g, 5)[0:NCMP_P, 0:P], ACT.Copy)
                        nc.scalar.activation(pt[par][1][:, 0:n], bank(g, 3)[:, 0:n], ACT.Copy).then_inc(t_act, 1)

        @block.tensor
        def _(pe):
            pe.sem_inc(scores, NU)
            pe.sem_inc(turned, NU)
            pe.sem_inc(o_mm, NU)
            with pe.Fori(0, GRP) as j:
                pe.wait_ge(q_ready, j + 1)
                for s in range(NU + 2):
                    if s < NU:
                        gg, qt = units[s]
                        half = slice(gg * HD, (gg + 1) * HD)
                        done(pe, biased, j, s - 1)
                        lhs = q[half, qt * P:(qt + 1) * P]
                        nc.tensor.matmul(bank(g, 2)[:, 0:NCMP_P], lhs, g.kc_p[half, :], start=True, stop=True)
                        for br in (1, 2):
                            last = nc.tensor.matmul(bank(g, br - 1)[:, 0:(qt + 1) * P], lhs, g.zT[half, KT[br], 0:(qt + 1) * P], start=True, stop=True)
                        last.then_inc(scores, 1)
                    if 1 <= s <= NU:
                        u = s - 1
                        gg, qt = units[u]
                        par = u % 2
                        done(pe, diags, j, u)
                        done(pe, t_act, j, u - 1)
                        done(pe, t_dve, j, u - 1)
                        nc.tensor.matmul(bank(g, 5)[0:NCMP_P, 0:P], ps_[par][0][:, :], diag[:, par, 0], start=True, stop=True)
                        for br in (1, 2):
                            for kb in range(qt + 1):
                                last = nc.tensor.matmul(bank(g, 2 + br)[:, kb * P:(kb + 1) * P], ps_[par][br][:, kb * P:(kb + 1) * P], diag[:, par, br],
                                                        start=True, stop=True)
                        last.then_inc(turned, 1)
                    if s >= 2:
                        u = s - 2
                        gg, qt = units[u]
                        par = u % 2
                        half = slice(gg * HD, (gg + 1) * HD)
                        done(pe, t_act, j, u)
                        done(pe, t_dve, j, u)
                        done(pe, o_out, j, u - 2)
                        out = bank(g, 6 + u % 2)[half, 0:P]
                        nc.tensor.matmul(out, g.vc_p[0:NCMP_P, half], pt[par][0][0:NCMP_P, :], start=True, stop=False)
                        for br in (1, 2):
                            for kb in range(qt + 1):
                                last = nc.tensor.matmul(out, V[br][:, kb, half], pt[par][br][:, kb * P:(kb + 1) * P],
                                                        start=False, stop=(br == 2 and kb == qt))
                        last.then_inc(o_mm, 1)


def attend_sample(nc, g):
    with ExitStack() as ctx:
        sb, sem = memory(nc, ctx)
        NS, NW_ = PAST + ST, WIN + ST
        qbd = sb("q_block_diag", [P, DB, 2, GRP, DS])
        ss = sb("s_sel", [P, NS])
        sw = sb("s_win", [P, NW_])
        sc = sb("s_cmp", [P, NCMP_S])
        pn = sb("p_norm", [P, NCMP_S])
        pt_ = sb("s_pt", [P, 15, P])
        mx = sb("s_mx", [P, 6])
        nm = sb("s_nm", [P, 3])
        rs = sb("s_rs", [P, 3])
        wt = sb("s_wt", [P, 3])
        gm = sb("s_gm", [P, 24])
        gr = sb("s_gr", [P, 3])
        ks, kw = sb("ks", [P, BPT, PAST]), sb("kw", [P, BPT, WIN])
        vs, vw = sb("vs", [P, BPT, NPAGE, P]), sb("vw", [P, BPT, 4, P])
        k_in, v_in = sem("cache_k_in"), sem("cache_v_in")
        imp = sb("s_imp", [P, NBLK])
        drop = sb("s_drop", [P, 4])
        pen = sb("s_pen", [P, NBLK])
        diag = sb("s_diag", [P, 3, P])
        zero, q_ready, c_mm, s_mm, e_cmp, imp_mm, e_all, bias_c, bias_all, norm_c, diags, t_mm, t_act, t_dve, o_mm, o_out, ch = map(sem, (
            "s_zero", "s_q_ready", "s_c_mm", "s_s_mm", "s_e_cmp", "s_imp_mm", "s_e_all", "s_bias_c", "s_bias_all", "s_norm_c",
            "s_diags", "s_t_mm", "s_t_act", "s_t_dve", "s_o_mm", "s_o_out", "s_chain"))
        block = ctx.enter_context(nc.Block())
        PIECES = [(k, P) for k in range(8)] + [(8, P), (9, P), (10, P), (11, P), (12, ST), (13, ST), (14, NCMP_S)]
        SRC = [(1, ss[:, k * P:(k + 1) * P]) for k in range(8)] + [(2, sw[:, k * P:(k + 1) * P]) for k in range(4)] + \
              [(1, ss[:, PAST:NS]), (2, sw[:, WIN:NW_]), (0, sc[:, :])]

        @block.gpsimd
        def _(pool):
            pool.memset(qbd[:, :, :, :, :], 0.0).then_inc(zero, 1)
            for bt in range(2):
                if bt:
                    pool.wait_ge(s_mm, 1)
                for b in range(BPT):
                    pool.dma_start(kw[:, b], g.a["cache_win_k"][bt * BPT + b]).then_inc(k_in, 16)
                for k in range(BPT * NPAGE):
                    page = pool.value_load(g.table[0:1, bt * BPT * NPAGE + k:bt * BPT * NPAGE + k + 1], min_val=0, max_val=NPHYS - 1)
                    pool.dma_start(ks[:, k // NPAGE, (k % NPAGE) * PAGE:(k % NPAGE + 1) * PAGE],
                                   g.a["cache_sel_k"][bass.ds(page, 1)].rearrange("a p n -> p (a n)")).then_inc(k_in, 16)

        @block.sync
        def _(sp):
            for bt in range(2):
                if bt:
                    sp.wait_ge(o_mm, 1)
                for b in range(BPT):
                    sp.dma_start(vw[:, b], g.a["cache_win_v"][bt * BPT + b]).then_inc(v_in, 16)
                for k in range(BPT * NPAGE):
                    page = sp.value_load(g.table[0:1, bt * BPT * NPAGE + k:bt * BPT * NPAGE + k + 1], min_val=0, max_val=NPHYS - 1)
                    sp.dma_start(vs[:, k // NPAGE, k % NPAGE], g.a["cache_sel_v"][bass.ds(page, 1)].rearrange("a p n -> p (a n)")).then_inc(v_in, 16)

        @block.vector
        def _(dve):
            chain = [0]

            def link(ins):
                chain[0] += 1
                ins.then_inc(ch, 1)
                dve.wait_ge(ch, chain[0])

            dve.wait_ge(zero, 1)
            for gg in range(KVH):
                half = slice(gg * HD, (gg + 1) * HD)
                for b in range(DB):
                    last = nc.vector.tensor_copy(qbd[half, b, gg], g.zT[half, 0:GRP, SEQ + DS * b:SEQ + DS * (b + 1)])
            last.then_inc(q_ready, 1)
            for bt in range(2):
                dve.wait_ge(c_mm, bt + 1)
                link(nc.vector.tensor_tensor(gm[:, :], bank(g, 4)[:, 64:88], g.c["c_gate_row"][:, :], ALU.mult))
                nc.vector.tensor_reduce(out=gr[:, :], in_=gm[:, :].rearrange("p (b x) -> p b x", b=3), axis=AX.X, op=ALU.add)
                link(nc.vector.tensor_tensor_reduce(out=sc[:, :], in0=bank(g, 3)[:, 64:64 + NCMP_S], in1=g.c["c_cmp_s"][:, :], scale=1.0, scalar=-3e38,
                                                    op0=ALU.add, op1=ALU.max, accum_out=mx[:, 0:1]))
                nc.vector.tensor_scalar(nm[:, 0:1], mx[:, 0:1], g.c["c_slope_s"][:, :], -1.0, ALU.mult, ALU.mult).then_inc(bias_c, 1)
                dve.wait_ge(s_mm, bt + 1)
                tail = g.c["c_tail_s"][:, bt * ST:(bt + 1) * ST]
                link(nc.vector.tensor_tensor_reduce(out=sw[:, 0:WIN], in0=bank(g, 2)[:, :], in1=g.c["c_win_s"][:, :], scale=1.0, scalar=-3e38,
                                                    op0=ALU.add, op1=ALU.max, accum_out=mx[:, 1:2]))
                link(nc.vector.tensor_tensor_reduce(out=sw[:, WIN:NW_], in0=bank(g, 3)[:, ST:2 * ST], in1=tail, scale=1.0, scalar=mx[:, 1:2],
                                                    op0=ALU.add, op1=ALU.max, accum_out=mx[:, 2:3]))
                nc.vector.tensor_scalar(nm[:, 2:3], mx[:, 2:3], g.c["c_slope_s"][:, :], -1.0, ALU.mult, ALU.mult)
                link(nc.vector.tensor_tensor(ss[:, 0:PAST], bank(g, 0, 2), g.c["c_sel_s"][:, :], ALU.add))
                dve.wait_ge(e_cmp, bt + 1)
                link(nc.vector.reciprocal(wt[:, 0:1], rs[:, 0:1]))
                nc.vector.tensor_scalar(pn[:, :], sc[:, :], wt[:, 0:1], None, ALU.mult).then_inc(norm_c, 1)
                dve.wait_ge(imp_mm, bt + 1)
                im = bank(g, 4)
                nc.vector.tensor_reduce(out=imp[:, 0:15], in_=im[:, 0:60].rearrange("p (k x) -> p k x", x=4), axis=AX.X, op=ALU.add)
                link(nc.vector.tensor_reduce(out=imp[:, 15:16], in_=im[:, 60:63], axis=AX.X, op=ALU.add))
                link(nc.vector.tensor_tensor(imp[:, 1:16], imp[:, 1:16], im[:, 3:63:4], ALU.add))
                link(nc.vector.tensor_reduce(out=drop[:, 0:1], in_=imp[:, 1:NBLK - 1], axis=AX.X, op=ALU.min))
                link(nc.vector.scalar_tensor_tensor(out=pen[:, 1:NBLK - 1], in0=imp[:, 1:NBLK - 1], scalar=drop[:, 0:1], in1=g.c["c_blk"][:, 1:NBLK - 1],
                                                    op0=ALU.is_equal, op1=ALU.mult))
                link(nc.vector.tensor_reduce(out=drop[:, 1:2], in_=pen[:, 1:NBLK - 1], axis=AX.X, op=ALU.max))
                link(nc.vector.tensor_scalar(pen[:, :], g.c["c_blk"][:, :], drop[:, 1:2], NEG, ALU.is_equal, ALU.mult))
                sv = ss[:, 0:PAST].rearrange("p (k x) -> p k x", x=SELB)
                link(nc.vector.tensor_tensor(sv, sv, pen[:, :, None].broadcast_to([P, NBLK, SELB]), ALU.add))
                link(nc.vector.tensor_reduce(out=mx[:, 3:4], in_=ss[:, 0:PAST], axis=AX.X, op=ALU.max))
                link(nc.vector.tensor_tensor_reduce(out=ss[:, PAST:NS], in0=bank(g, 3)[:, 0:ST], in1=tail, scale=1.0, scalar=mx[:, 3:4],
                                                    op0=ALU.add, op1=ALU.max, accum_out=mx[:, 4:5]))
                nc.vector.tensor_scalar(nm[:, 1:2], mx[:, 4:5], g.c["c_slope_s"][:, :], -1.0, ALU.mult, ALU.mult).then_inc(bias_all, 1)
                dve.wait_ge(e_all, bt + 1)
                link(nc.vector.reciprocal(wt[:, :], rs[:, :]))
                link(nc.vector.tensor_tensor(wt[:, :], wt[:, :], gr[:, :], ALU.mult))
                for br in range(3):
                    last = nc.vector.tensor_scalar(diag[:, br], g.c["c_ident"][:, :], wt[:, br:br + 1], None, ALU.mult)
                last.then_inc(diags, 1)
                dve.wait_ge(t_mm, bt + 1)
                nc.vector.tensor_copy(pt_[:, 8:12], bank(g, 2).rearrange("p (k n) -> p k n", k=4))
                nc.vector.tensor_copy(pt_[0:ST, 12:14], bank(g, 3)[0:ST, 0:2 * P].rearrange("p (k n) -> p k n", k=2))
                nc.vector.tensor_copy(pt_[0:NCMP_S, 14], bank(g, 3)[0:NCMP_S, 2 * P:3 * P]).then_inc(t_dve, 1)
                dve.wait_ge(o_mm, bt + 1)
                for gg in range(KVH):
                    half = slice(gg * HD, (gg + 1) * HD)
                    src = bank(g, 5)[half, 0:P].rearrange("p (b g j t) -> p g b j t", b=BPT, g=KVH, j=GRP)[:, gg]
                    for b in range(BPT):
                        at = SEQ + DS * (BPT * bt + b)
                        last = nc.vector.tensor_copy(g.mixT[half, 0:GRP, at:at + DS], src[:, b])
                last.then_inc(o_out, 1)

        @block.scalar
        def _(act):
            for bt in range(2):
                act.wait_ge(bias_c, bt + 1)
                nc.scalar.activation(sc[:, :], sc[:, :], ACT.Exp, bias=nm[:, 0:1], scale=g.c["c_slope_s"][:, :], accum_out=rs[:, 0:1]).then_inc(e_cmp, 1)
                act.wait_ge(bias_all, bt + 1)
                nc.scalar.activation(sw[:, :], sw[:, :], ACT.Exp, bias=nm[:, 2:3], scale=g.c["c_slope_s"][:, :], accum_out=rs[:, 2:3])
                nc.scalar.activation(ss[:, :], ss[:, :], ACT.Exp, bias=nm[:, 1:2], scale=g.c["c_slope_s"][:, :], accum_out=rs[:, 1:2]).then_inc(e_all, 1)
                act.wait_ge(t_mm, bt + 1)
                nc.scalar.activation(pt_[:, 0:8], bank(g, 0, 2).rearrange("p (k n) -> p k n", k=8), ACT.Copy).then_inc(t_act, 1)

        @block.tensor
        def _(pe):
            pe.wait_ge(q_ready, 1)
            qv = lambda b: qbd[:, b].rearrange("p g j t -> p (g j t)")
            for bt in range(2):
                b0 = BPT * bt
                if bt:
                    pe.wait_ge(t_dve, bt)
                    pe.wait_ge(t_act, bt)
                rows = qbd[:, b0:b0 + BPT].rearrange("p b g j t -> p (b g j t)")
                nc.tensor.matmul(bank(g, 3)[:, 0:ST], rows, g.zT[:, 6, SEQ:T], start=True, stop=True)
                nc.tensor.matmul(bank(g, 3)[:, ST:2 * ST], rows, g.zT[:, 8, SEQ:T], start=True, stop=True)
                for b in range(BPT):
                    nc.tensor.matmul(bank(g, 3)[32 * b:32 * b + 32, 64:64 + NCMP_S], qv(b0 + b), g.kc_s[:, b0 + b], start=True, stop=True)
                nc.tensor.matmul(bank(g, 4)[:, 64:88], g.c["c_tok_row"][0:ST, bt * ROWS:(bt + 1) * ROWS], g.gates[0:ST, 4], start=True, stop=True).then_inc(c_mm, 1)
                pe.wait_ge(k_in, 16 * BPT * (NPAGE + 1) * (bt + 1))
                for b in range(BPT):
                    r = slice(32 * b, 32 * b + 32)
                    for h in range(2):
                        nc.tensor.matmul(bank(g, h)[r, :], qv(b0 + b), ks[:, b, 512 * h:512 * h + 512], start=True, stop=True)
                    last = nc.tensor.matmul(bank(g, 2)[r, :], qv(b0 + b), kw[:, b], start=True, stop=True)
                last.then_inc(s_mm, 1)
                pe.wait_ge(norm_c, bt + 1)
                nc.tensor.matmul(bank(g, 4)[:, 0:NCMP_S], g.c["c_same_bgt"][:, :], pn[:, :], start=True, stop=True).then_inc(imp_mm, 1)
                pe.wait_ge(diags, bt + 1)
                for k, (br, src) in enumerate(SRC):
                    m = PIECES[k][1]
                    at = bank(g, k // 4)[0:m, (k % 4) * P:(k % 4 + 1) * P]
                    last = nc.tensor.matmul(at, src, diag[:, br], start=True, stop=True)
                last.then_inc(t_mm, 1)
                pe.wait_ge(v_in, 16 * BPT * (NPAGE + 1) * (bt + 1))
                pe.wait_ge(t_act, bt + 1)
                pe.wait_ge(t_dve, bt + 1)
                if bt:
                    pe.wait_ge(o_out, bt)
                for b in range(BPT):
                    cols = slice(32 * b, 32 * b + 32)
                    values = [vs[:, b, k] for k in range(8)] + [vw[:, b, k] for k in range(4)] + \
                         [g.v_sel[0:ST, 4], g.v_win[0:ST, 4], g.vc_s[0:NCMP_S, b0 + b]]
                    for k, v in enumerate(values):
                        last = nc.tensor.matmul(bank(g, 5)[:, cols], v, pt_[0:PIECES[k][1], k, cols], start=(k == 0), stop=(k == 14))
                last.then_inc(o_mm, 1)


def output(nc, g):
    with ExitStack() as ctx:
        sb, sem = memory(nc, ctx)
        w = [sb(f"wo_tile{k}", [P, KC * P]) for k in range(2)]
        w_in = [sem("wo_in0"), sem("wo_in1")]
        o_mm, h_out = sem("o_proj"), sem("h_out")
        block = ctx.enter_context(nc.Block())

        @block.gpsimd
        def _(pool):
            for i in range(KC):
                if i >= 2:
                    pool.wait_ge(o_mm, i - 1)
                pool.dma_start(w[i % 2][:, :], g.a["w_out"][i]).then_inc(w_in[i % 2], 16)

        @block.tensor
        def _(pe):
            with pe.Fori(0, KC // 2) as i:
                for par in range(2):
                    pe.wait_ge(w_in[par], 16 * i + 16)
                    pe.wait_ge(h_out, 2 * i + (par + 1))
                    for h in range(2):
                        for k in range(KC):
                            last = nc.tensor.matmul(bank(g, 2 * par + h)[:, 0:HALF], w[par][:, k * P:(k + 1) * P],
                                                    g.mixT[:, k, h * HALF:(h + 1) * HALF], start=(k == 0), stop=(k == KC - 1))
                    last.then_inc(o_mm, 1)

        @block.vector
        def _(dve):
            dve.sem_inc(h_out, 2)
            with dve.Fori(0, KC // 2) as i:
                for par in range(2):
                    dve.wait_ge(o_mm, 2 * i + (par + 1))
                    ht = g.xT[:, bass.ds(2 * i + par, 1)].rearrange("p a (h n) -> p (a h) n", h=2)
                    nc.vector.tensor_tensor(ht, ht, bank(g, 2 * par, 2).rearrange("p (h n) -> p h n", h=2)[:, :, 0:HALF], ALU.add).then_inc(h_out, 1)


def queries(nc, g):
    with ExitStack() as ctx:
        sb, sem = memory(nc, ctx)
        NQ = 2 * PH
        w = [sb(f"wq_tile{k}", [P, KC * P]) for k in range(2)]
        keys = sb("sub_keys", [P, NQ, NKEY])
        sq = sb("sq2", [P, 2, T])
        rstd = sb("rstd2", [P, T])
        norm2 = sb("norm2", [P, KC])
        xn = sb("xn2", [P, KC, T])
        qp = sb("q_peer", [P, 2, T])
        w_in = [sem("wq_in0"), sem("wq_in1")]
        n_in, sq_ready, sq_used, std_ready, rstd_ready, xn_ready, hi_ready = map(sem, (
            "n2_in", "sq2_ready", "sq2_used", "std2_ready", "rstd2_ready", "xn2_ready", "hi_ready"))
        q_mm, q_act, q_dve, s_mm, s_act, s_dve = map(sem, ("q_mm", "q_act", "q_dve", "ps_mm", "ps_act", "ps_dve"))
        block = ctx.enter_context(nc.Block())

        @block.sync
        def _(sp):
            sp.dma_start(norm2[:, :], g.a["norm2"]).then_inc(n_in, 16)
            sp.dma_start(keys[:, :, :], g.a["subkeys"]).then_inc(n_in, 16)

        @block.gpsimd
        def _(pool):
            for i in range(NQ):
                if i >= 2:
                    pool.wait_ge(q_mm, i - 1)
                pool.dma_start(w[i % 2][:, :], g.a["peer_wq"][i]).then_inc(w_in[i % 2], 16)

        @block.tensor
        def _(pe):
            pe.wait_ge(n_in, 32)
            for k in range(KC):
                pe.wait_ge(sq_ready, k + 1)
                for h in range(2):
                    last = nc.tensor.matmul(bank(g, 4 + h)[:, 0:HALF], g.c["c_mean_d"][:, :], sq[:, k % 2, h * HALF:(h + 1) * HALF],
                                            start=(k == 0), stop=(k == KC - 1))
                last.then_inc(sq_used, 1)
            pe.wait_ge(xn_ready, KC)

            def project(par):
                for h in range(2):
                    for k in range(KC):
                        last = nc.tensor.matmul(bank(g, 2 * par + h)[:, 0:HALF], w[par][:, k * P:(k + 1) * P],
                                                xn[:, k, h * HALF:(h + 1) * HALF], start=(k == 0), stop=(k == KC - 1))
                last.then_inc(q_mm, 1)

            def score(i, par):
                pe.wait_ge(q_act, 2 * i + (par + 3))
                pe.wait_ge(q_dve, 2 * i + (par + 3))
                pe.wait_ge(s_act, 2 * i + (par + 1))
                pe.wait_ge(s_dve, 2 * i + (par + 1))
                key = keys[:, bass.ds(2 * i + par, 1)].rearrange("p a n -> p (a n)")
                for tt in range(QT):
                    nc.tensor.matmul(bank(g, 4 + par)[:, tt * P:(tt + 1) * P], qp[:, par, tt * P:(tt + 1) * P], key, start=True, stop=True)
                nc.tensor.matmul(bank(g, 6 + par)[0:ST, 0:NKEY], qp[:, par, SEQ:T], key, start=True, stop=True).then_inc(s_mm, 1)

            with pe.Fori(0, NQ // 2) as i:
                for par in range(2):
                    pe.wait_ge(w_in[par], 16 * i + 16)
                    pe.wait_ge(q_act, 2 * i + (par + 1))
                    pe.wait_ge(q_dve, 2 * i + (par + 1))
                    project(par)
                score(i, 0)
                score(i, 1)

        @block.vector
        def _(dve):
            dve.wait_ge(n_in, 32)
            dve.wait_ge(std_ready, 1)
            nc.vector.reciprocal(rstd[:, :], rstd[:, :]).then_inc(rstd_ready, 1)
            dve.wait_ge(rstd_ready, 1)
            for k in range(KC):
                nc.vector.scalar_tensor_tensor(out=xn[:, k], in0=g.xT[:, k], scalar=norm2[:, k:k + 1], in1=rstd[:, :],
                                               op0=ALU.mult, op1=ALU.mult).then_inc(xn_ready, 1)
            nc.vector.memset(g.S[:, 4], 0.0)
            dve.sem_inc(q_dve, 2)
            dve.sem_inc(s_dve, 2)
            with dve.Fori(0, NQ // 2) as i:
                for par in range(2):
                    dve.wait_ge(q_mm, 2 * i + (par + 1))
                    nc.vector.tensor_copy(qp[:, par, HALF:T], bank(g, 2 * par + 1)[:, 0:HALF]).then_inc(q_dve, 1)
                for par in range(2):
                    dve.wait_ge(s_mm, 2 * i + (par + 1))
                    nc.vector.tensor_copy(g.S[0:ST, 4, bass.ds(2 * i + par, 1)], bank(g, 6 + par)[0:ST, None, 0:NKEY]).then_inc(s_dve, 1)
            dve.wait_ge(hi_ready, 1)
            nc.vector.tensor_tensor(g.x_lo[:, :, :], xn[:, :, :], g.x_hi[:, :, :], ALU.subtract)

        @block.scalar
        def _(act):
            for k in range(KC):
                if k >= 2:
                    act.wait_ge(sq_used, k - 1)
                nc.scalar.activation(sq[:, k % 2], g.xT[:, k], ACT.Square).then_inc(sq_ready, 1)
            act.wait_ge(sq_used, KC)
            nc.scalar.activation(halves(rstd[:, :]), halves(bank(g, 4, 2))[:, :, 0:HALF], ACT.Sqrt, bias=g.c["c_eps"][:, :]).then_inc(std_ready, 1)
            act.sem_inc(q_act, 2)
            act.sem_inc(s_act, 2)
            with act.Fori(0, NQ // 2) as i:
                for par in range(2):
                    act.wait_ge(q_mm, 2 * i + (par + 1))
                    nc.scalar.activation(qp[:, par, 0:HALF], bank(g, 2 * par)[:, 0:HALF], ACT.Copy).then_inc(q_act, 1)
                for par in range(2):
                    act.wait_ge(s_mm, 2 * i + (par + 1))
                    nc.scalar.activation(g.S[:, 0:QT, bass.ds(2 * i + par, 1)], bank(g, 4 + par).rearrange("p (t a n) -> p t a n", t=QT, a=1), ACT.Copy).then_inc(s_act, 1)
            act.wait_ge(xn_ready, KC)
            nc.scalar.activation(g.x_hi[:, :, :], xn[:, :, :], ACT.Copy).then_inc(hi_ready, 1)


def retrieve(nc, g):
    with ExitStack() as ctx:
        sb, sem = memory(nc, ctx)
        NHC = 2 * PH
        rest = sb("rest", [P, NHC, NKEY])
        sv = sb("sv", [P, NHC, TOPK])
        si = sb("si", [P, NHC, TOPK], U32)
        sif = sb("sif", [P, NHC, TOPK])
        cand = sb("cand", [P, PH, TOPK * TOPK])
        crest = sb("crest", [P, PH, TOPK * TOPK])
        cv = sb("cv", [P, PH, TOPK])
        ci = sb("ci", [P, PH, TOPK], U32)
        cab = sb("cab", [P, 2, PH, TOPK], U32)
        cabf = sb("cabf", [P, 2, PH, TOPK])
        hot = sb("hot", [P, PH, TOPK, TOPK])
        slot = sb("slot", [P, 3, PH, TOPK])
        cur_s = sb("cur_s", [P, NHC, NKEY])
        cexp = sb("cexp", [P, PH, TOPK])
        sm = sb("sm", [P, PH])
        ri = sb("ri", [P, PH])
        slotT = sb("slotT", [P, 3, NTT * P])
        stage = sb("slot_stage", [P, 2, 3, 32])
        oh = [[sb(f"one_hot{n}{k}", [P, 4, P]) for k in range(2)] for n in range(2)]
        gst = [sb(f"g_stage{k}", [P, NKEY, 32]) for k in range(2)]
        ch, tr_ready, tr_mm, tr_out, e_in, e_out = map(sem, ("r_chain", "tr_ready", "r_tr_mm", "r_tr_out", "r_e_in", "r_e_out"))
        started = sem("r_started")
        staged, hots, keys, g_mm, g_out, g_stored = map(sem, ("staged", "hots", "keys", "g_mm", "g_out", "g_stored"))
        stored = [sem("g_stored0"), sem("g_stored1")]
        block = ctx.enter_context(nc.Block())
        NCH = T // 32

        LINKS = 19

        @block.vector
        def _(dve):
            with dve.Fori(0, NTT) as tt:
                at = [0]

                def link(ins):
                    at[0] += 1
                    ins.then_inc(ch, 1)
                    dve.wait_ge(ch, LINKS * tt + at[0])

                def link_max(ins):
                    link(ins)
                    dve.sem_inc(started, 1)

                S = g.S[:, bass.ds(tt, 1)].rearrange("p a k n -> p (a k) n")
                link_max(nc.vector.tensor_copy(cur_s[:, :, :], S))
                for k in range(NHC):
                    last = nc.vector.max(out=sv[:, k, 0:8], in_=cur_s[:, k])
                link_max(last)
                for k in range(NHC):
                    nc.vector.max_index(out=si[:, k, 0:8], in_max=sv[:, k, 0:8], in_values=cur_s[:, k])
                    last = nc.vector.match_replace(out=rest[:, k], in_to_replace=sv[:, k, 0:8], in_values=cur_s[:, k], imm_value=-3e38)
                link_max(last)
                for k in range(NHC):
                    last = nc.vector.max(out=sv[:, k, 8:16], in_=rest[:, k])
                link_max(last)
                for k in range(NHC):
                    nc.vector.max_index(out=si[:, k, 8:16], in_max=sv[:, k, 8:16], in_values=rest[:, k])
                v = sv[:, :, :].rearrange("p (h c) k -> p h c k", c=2)
                for h in range(PH):
                    last = nc.vector.tensor_tensor(cand[:, h].rearrange("p (a b) -> p a b", a=TOPK), v[:, h, 0][:, :, None].broadcast_to([P, TOPK, TOPK]),
                                                   v[:, h, 1][:, None, :].broadcast_to([P, TOPK, TOPK]), ALU.add)
                link_max(last)
                for h in range(PH):
                    last = nc.vector.max(out=cv[:, h, 0:8], in_=cand[:, h])
                link_max(last)
                for h in range(PH):
                    nc.vector.max_index(out=ci[:, h, 0:8], in_max=cv[:, h, 0:8], in_values=cand[:, h])
                    last = nc.vector.match_replace(out=crest[:, h], in_to_replace=cv[:, h, 0:8], in_values=cand[:, h], imm_value=-3e38)
                link_max(last)
                for h in range(PH):
                    last = nc.vector.max(out=cv[:, h, 8:16], in_=crest[:, h])
                link_max(last)
                for h in range(PH):
                    last = nc.vector.max_index(out=ci[:, h, 8:16], in_max=cv[:, h, 8:16], in_values=crest[:, h])
                link(last)
                nc.vector.tensor_tensor(cexp[:, :, :], cv[:, :, :], cv[:, :, 0:1].broadcast_to([P, PH, TOPK]), ALU.subtract).then_inc(e_in, 1)
                nc.vector.tensor_scalar(cab[:, 0], ci[:, :, :], 4, None, ALU.logical_shift_right)
                nc.vector.tensor_scalar(cab[:, 1], ci[:, :, :], 15, None, ALU.bitwise_and)
                link(nc.vector.tensor_copy(sif[:, :, :], si[:, :, :]))
                link(nc.vector.tensor_copy(cabf[:, :, :, :], cab[:, :, :, :]))
                dve.wait_ge(tr_mm, tt + 1)
                sf = sif[:, :, :].rearrange("p (h c) k -> p h c k", c=2)
                io = g.c["c_iota"][:, 0:TOPK]
                for c in range(2):
                    hv = hot[:, :, :, :].rearrange("p h k r -> p (h k) r")
                    link(nc.vector.tensor_tensor(hv, cabf[:, c].rearrange("p h k -> p (h k)")[:, :, None].broadcast_to([P, P, TOPK]),
                                                 io[:, None, :].broadcast_to([P, P, TOPK]), ALU.is_equal))
                    for h in range(PH):
                        last = nc.vector.tensor_tensor(hot[:, h], hot[:, h], sf[:, h, c][:, None, :].broadcast_to([P, TOPK, TOPK]), ALU.mult)
                    link(last)
                    link(nc.vector.tensor_reduce(out=slot[:, c].rearrange("p h k -> p (h k)"), in_=hv, axis=AX.X, op=ALU.add))
                dve.wait_ge(e_out, tt + 1)
                link(nc.vector.tensor_reduce(out=sm[:, :], in_=cexp[:, :, :], axis=AX.X, op=ALU.add))
                link(nc.vector.reciprocal(ri[:, :], sm[:, :]))
                nc.vector.tensor_tensor(slot[:, 2], cexp[:, :, :], ri[:, :, None].broadcast_to([P, PH, TOPK]), ALU.mult).then_inc(tr_ready, 1)
                assert at[0] == LINKS, at[0]
            dve.wait_ge(tr_out, NTT)
            dve.sem_inc(hots, 8)
            with dve.Fori(0, NCH) as c:
                dve.wait_ge(hots, 8 * c + 8)
                nc.vector.tensor_copy(stage[:, 0], slotT[:, :, bass.ds(32 * c, 32)]).then_inc(staged, 1)
                dve.wait_ge(staged, c + 1)
                for q in range(8):
                    dve.wait_ge(g_mm, 8 * c + (8 + q - 1))
                    for t in range(4):
                        k = 4 * q + t
                        nc.vector.tensor_scalar(oh[0][q % 2][:, t], g.c["c_iota"][:, :], stage[:, 0, 0, k:k + 1], None, ALU.is_equal)
                        last = nc.vector.tensor_scalar(oh[1][q % 2][:, t], g.c["c_iota"][:, :], stage[:, 0, 1, k:k + 1], stage[:, 0, 2, k:k + 1], ALU.is_equal, ALU.mult)
                    last.then_inc(hots, 1)

        @block.scalar
        def _(act):
            with act.Fori(0, NTT) as tt:
                act.wait_ge(e_in, tt + 1)
                nc.scalar.activation(cexp[:, :, :], cexp[:, :, :], ACT.Exp).then_inc(e_out, 1)
                act.wait_ge(tr_mm, tt + 2)
                nc.scalar.activation(slotT[:, :, bass.ds(P * tt, P)], bank(g, 7)[:, 0:3 * P].rearrange("p (k n) -> p k n", k=3), ACT.Copy).then_inc(tr_out, 1)
            act.sem_inc(g_out, 8)
            with act.Fori(0, NCH // 2) as cc:
                for par in range(2):
                    act.wait_ge(stored[par], 16 * cc + 16)
                    for q in range(8):
                        act.wait_ge(g_mm, 16 * cc + (8 * par + 8 + q + 1))
                        nc.scalar.activation(gst[par][:, :, 4 * q:4 * q + 4], bank(g, q % 4).rearrange("p (t i) -> p i t", t=4), ACT.Copy).then_inc(g_out, 1)
            act.wait_ge(stored[0], 16 * (NCH // 2) + 16)
            for q in range(8):
                act.wait_ge(g_mm, 8 * (NCH - 1) + 8 + q + 1)
                nc.scalar.activation(gst[0][:, :, 4 * q:4 * q + 4], bank(g, q % 4).rearrange("p (t i) -> p i t", t=4), ACT.Copy).then_inc(g_out, 1)

        @block.tensor
        def _(pe):
            pe.sem_inc(tr_mm, 1)
            with pe.Fori(0, NTT) as tt:
                pe.wait_ge(tr_ready, tt + 1)
                for k in range(3):
                    last = nc.tensor.transpose(bank(g, 7)[:, k * P:(k + 1) * P], slot[:, k].rearrange("p h k -> p (h k)"), g.c["c_ident"][:, :])
                last.then_inc(tr_mm, 1)
                pe.wait_ge(tr_out, tt + 1)
            pe.sem_inc(g_mm, 8)
            with pe.Fori(0, NCH) as c:
                for q in range(8):
                    pe.wait_ge(hots, 8 * c + (8 + q + 1))
                    pe.wait_ge(g_out, 8 * c + (8 + q + 1 - 4))
                    for t in range(4):
                        last = nc.tensor.matmul(bank(g, q % 4)[:, t * P:(t + 1) * P], oh[1][q % 2][:, t], oh[0][q % 2][:, t], start=True, stop=True)
                    last.then_inc(g_mm, 1)

        @block.sync
        def _(sp):
            sp.sem_inc(stored[0], 16)
            sp.sem_inc(stored[1], 16)
            for c in range(NCH):
                sp.wait_ge(g_out, 8 * c + 16)
                sp.dma_start(g.a["gates_dense"][c], gst[c % 2][:, :, :].rearrange("p i t -> p (i t)")).then_inc(stored[c % 2], 16)
            sp.wait_ge(stored[0], 16 + 16 * ((NCH + 1) // 2))
            sp.wait_ge(stored[1], 16 + 16 * (NCH // 2))


def experts(nc, g):
    with ExitStack() as ctx:
        sb, sem = memory(nc, ctx)
        NUN = GE + KC
        NCH = T // 32
        raw = [sb(f"raw{k}", [P, KC * P]) for k in range(2)]
        whi = [sb(f"w_hi{k}", [P, KC * P], F32R) for k in range(2)]
        wlo = [sb(f"w_lo{k}", [P, KC * P], F32R) for k in range(2)]
        c_hi = sb("c_hi", [P, GE, T], F32R)
        c_lo = sb("c_lo", [P, GE, T], F32R)
        gates = sb("gates_g", [P, NCH, GE * 32])
        hid = sb("hid", [P, 2, T])
        cf = sb("cf", [P, 2, T])
        raw_in = [sem("raw_in0"), sem("raw_in1")]
        w_hi, w_lo, mm, gelu, mul, c_h, c_l, acc, gates_in, y_out = map(sem, ("w_hi", "w_lo", "mm", "gelu", "mul", "c_h", "c_l", "acc", "gates_in", "y_out"))
        block = ctx.enter_context(nc.Block())

        def groups(eng, body):
            with eng.Fori(0, NG - 1) as n:
                body(n, False)
            body(NG - 1, True)

        @block.sync
        def _(sp):
            with sp.Fori(0, NG) as n:
                for k in range(NUN):
                    arr, at = ("expert_u", GE * n + k) if k < GE else ("expert_v", KC * n + (k - GE))
                    src = g.a[arr][bass.ds(at, 1)].rearrange("a p n -> p (a n)")
                    sp.wait_ge(w_lo, NUN * n + (k + 1))
                    sp.dma_start(raw[k % 2][:, :], src).then_inc(raw_in[k % 2], 16)
            sp.wait_ge(acc, KC * NG + 2)
            sp.dma_start(g.a["out_y"], g.xT[:, :, :]).then_inc(y_out, 16)
            sp.wait_ge(y_out, 16)

        @block.gpsimd
        def _(pool):
            with pool.Fori(0, NG) as n:
                pool.wait_ge(mul, GE * n + GE)
                pool.dma_start(gates[:, :, :], g.a["gates_dense"].rearrange("c p n -> p c n")[:, :, bass.ds(GE * 32 * n, GE * 32)]).then_inc(gates_in, 16)

        @block.scalar
        def _(act):
            def split(n, k):
                act.wait_ge(raw_in[k % 2], 16 * (NUN // 2) * n + 16 * (k // 2 + 1))
                act.wait_ge(mm, NUN * n + (k + 1))
                nc.scalar.activation(whi[k % 2][:, :], raw[k % 2][:, :], ACT.Copy).then_inc(w_hi, 1)

            def body(n, last):
                for k in range(NUN):
                    if not (last and k == NUN - 1):
                        split(n, k + 1)
                    if k < GE:
                        act.wait_ge(mm, NUN * n + (k + 3))
                        act.wait_ge(mul, GE * n + (GE + k - 1))
                        nc.scalar.activation(halves(hid[:, k % 2]), halves(bank(g, 2 * (k % 2), 2))[:, :, 0:HALF], ACT.Gelu_apprx_tanh).then_inc(gelu, 1)
                        act.wait_ge(mul, GE * n + (GE + k + 1))
                        nc.scalar.activation(c_hi[:, k], cf[:, k % 2], ACT.Copy).then_inc(c_h, 1)

            act.sem_inc(gelu, 2)
            split(0, 0)
            groups(act, body)

        @block.vector
        def _(dve):
            def split(n, k):
                dve.wait_ge(w_hi, NUN * n + (k + 1))
                dve.wait_ge(mm, NUN * n + (k + 1))
                nc.vector.tensor_tensor(wlo[k % 2][:, :], raw[k % 2][:, :], whi[k % 2][:, :], ALU.subtract).then_inc(w_lo, 1)

            def body(n, last):
                for k in range(NUN):
                    if not (last and k == NUN - 1):
                        split(n, k + 1)
                    if k < GE:
                        if k == 0:
                            dve.wait_ge(gates_in, 16 * n + 16)
                        dve.wait_ge(gelu, GE * n + (k + 3))
                        tok = lambda x: x.rearrange("p (c t) -> p c t", t=32)
                        nc.vector.tensor_tensor(tok(cf[:, k % 2]), tok(hid[:, k % 2]), gates[:, :, 32 * k:32 * k + 32], ALU.mult).then_inc(mul, 1)
                        dve.wait_ge(c_h, GE * n + (k + 1))
                        nc.vector.tensor_tensor(c_lo[:, k], cf[:, k % 2], c_hi[:, k], ALU.subtract).then_inc(c_l, 1)
                    else:
                        m = k - GE
                        dve.wait_ge(mm, NUN * n + (k + 3))
                        nc.vector.tensor_tensor(halves(g.xT[:, m]), halves(g.xT[:, m]), halves(bank(g, 4 + 2 * (k % 2), 2))[:, :, 0:HALF], ALU.add).then_inc(acc, 1)

            dve.sem_inc(w_lo, 2)
            dve.sem_inc(mul, GE)
            dve.sem_inc(acc, 2)
            split(0, 0)
            groups(dve, body)

        @block.tensor
        def _(pe):
            pe.sem_inc(mm, 2)
            with pe.Fori(0, NG) as n:
                for k in range(NUN):
                    hi, lo = whi[k % 2], wlo[k % 2]
                    pe.wait_ge(w_lo, NUN * n + (k + 3))
                    if k < GE:
                        pe.wait_ge(gelu, GE * n + (k + 1))
                    else:
                        pe.wait_ge(acc, KC * n + (k - GE + 1))
                    for c in range(8):
                        if k == GE:
                            pe.wait_ge(c_l, GE * n + (c + 1))
                        for st, mv in ((hi, 0), (hi, 1), (lo, 0)):
                            for h in range(2):
                                cols = slice(h * HALF, (h + 1) * HALF)
                                if k < GE:
                                    out, mov = bank(g, 2 * (k % 2) + h), (g.x_hi, g.x_lo)[mv][:, c, cols]
                                else:
                                    out, mov = bank(g, 4 + 2 * (k % 2) + h), (c_hi, c_lo)[mv][:, c, cols]
                                last = nc.tensor.matmul(out[:, 0:HALF], st[:, c * P:(c + 1) * P], mov,
                                                        start=(c == 0 and st is hi and mv == 0), stop=(c == 7 and st is lo))
                    last.then_inc(mm, 1)


OUTS = {
    "out_kv": ((P, 6, T), F32), "out_u": ((P, 4, PST + ST), F32),
    "out_win_past": ((DB, (WIN - DS) * 2 * P), F32), "out_pool_past": ((DB, (PST - DS) * 512), F32),
    "out_y": ((P, KC, T), F32),
}


def prepare(inputs):
    f = lambda x: np.ascontiguousarray(np.asarray(x))
    i = {k: np.asarray(v) for k, v in inputs.items()}
    a = dict(constants())
    x = np.concatenate([i["x_prompt"].reshape(SEQ, D), i["x_sample"].reshape(ST, D)], 0)
    a["xT"] = f(x.T.reshape(KC, P, T).transpose(1, 0, 2))
    a["norm1"] = f(i["norm1_g"][0].reshape(KC, P).T)
    a["norm2"] = f(i["norm2_g"][0].reshape(KC, P).T)
    q, k = i["q_norm_g"][0], i["k_norm_g"][0]
    a["head_gains"] = f(np.stack([np.tile(v, 2) for v in (q, k[0], k[1], k[2])], 1))
    w = i["w_in"][0]
    wq = w[:, :512].reshape(D, KVH, GRP, HD).transpose(0, 2, 1, 3).reshape(D, 512)
    cols = np.concatenate([wq, w[:, 512:1280], w[:, 1304:1816]], 1)
    a["w_in"] = f(cols.reshape(KC, P, NZT, P).transpose(2, 1, 0, 3).reshape(NZT, P, KC * P))
    a["w_gate"] = f(w[:, 1280:1304].reshape(KC, P, 24).transpose(1, 0, 2))
    w1 = i["cmp_w1"][0].reshape(2, 2, 2, 8, HD, 128)
    a["cmp_w1"] = f(w1.transpose(2, 4, 0, 1, 3, 5).reshape(P, -1))
    a["cmp_w2"] = f(i["cmp_w2"][0].transpose(1, 0, 2).reshape(P, -1))
    pos = i["cmp_pos"][0].reshape(2, 2, 2, 8, HD)
    a["cmp_pos"] = f(pos.transpose(2, 4, 0, 1, 3).reshape(P, -1))
    cc = i["cache_cmp"][0].reshape(NPHYS, 8, 2, 8, 2, 2, HD)
    a["cache_cmp"] = f(cc.transpose(0, 2, 6, 4, 5, 3, 1).reshape(NPHYS, P, -1))
    cs = i["cache_sel"][0]
    a["cache_sel_k"] = f(cs[:, :, 0].reshape(NPHYS, PAGE, P).transpose(0, 2, 1))
    a["cache_sel_v"] = f(cs[:, :, 1].reshape(NPHYS, PAGE, P))
    cw = i["cache_win"][0]
    a["cache_win_k"] = f(cw[:, :, 0].reshape(DB, WIN, P).transpose(0, 2, 1))
    a["cache_win_v"] = f(cw[:, :, 1].reshape(DB, 4, P, P).transpose(0, 2, 1, 3))
    a["cache_win_kept"] = f(cw[:, DS:].reshape(DB, -1))
    a["state_pool_kept"] = f(i["state_pool"][0][:, DS:].reshape(DB, -1))
    a["state_pool_t"] = f(i["state_pool"][0].reshape(DB, PST, 4, P).transpose(3, 2, 0, 1))
    a["page_table"] = f(i["page_table"].reshape(1, -1))
    a["pool_w"] = f(i["pool_w"][0].transpose(1, 0, 2))
    a["pool_scale"] = f(i["pool_scale"][0].reshape(4, P).T)
    wo = i["w_out"][0]
    wo = np.concatenate([wo[:512].reshape(KVH, GRP, HD, D).transpose(1, 0, 2, 3).reshape(512, D), wo[512:]], 0)
    a["w_out"] = f(wo.reshape(KC, P, KC, P).transpose(2, 1, 0, 3).reshape(KC, P, KC * P))
    a["peer_wq"] = f(i["peer_wq"][0].reshape(KC, P, 16, P).transpose(2, 1, 0, 3).reshape(16, P, KC * P))
    a["subkeys"] = f(i["peer_subkeys"][0].reshape(16, NKEY, P).transpose(2, 0, 1))
    eu = i["expert_u"][0].reshape(NKEY, NKEY, KC, P)
    a["expert_u"] = f(eu.transpose(0, 3, 2, 1).reshape(NKEY, P, KC * P))
    ev = i["expert_v"][0].reshape(NG, GE, P, KC, P)
    a["expert_v"] = f(ev.transpose(0, 3, 2, 1, 4).reshape(NG * KC, P, GE * P))
    return a


def build(nc, a):
    with ExitStack() as ctx:
        sb, sem = memory(nc, ctx)
        g = Shared()
        g.a, g.c = a, {}
        g.ps = ctx.enter_context(nc.psum_tensor("ps", [P, 4096], F32))
        for n in a:
            if n.startswith("c_"):
                g.c[n] = sb(n + "_sb", list(a[n].shape))
        g.xT = sb("xT_sb", [P, KC, T])
        with ExitStack() as front:
            fs, _ = memory(nc, front)
            g.gates = fs("gates_sb", [P, NTT, 3 * NH])
            g.kc_gain = fs("kc_gain", [P, 1])
            g.table = fs("page_table_sb", [1, DB * NPAGE], I32)
            g.zT = fs("zT", [P, NZT, T])
            project(nc, g)
            g.v_sel, g.v_win = fs("v_sel", [P, NTT, P]), fs("v_win", [P, NTT, P])
            g.kc_p, g.vc_p = fs("kc_p", [P, NCMP_P]), fs("vc_p", [P, P])
            g.kc_s, g.vc_s = fs("kc_s", [P, DB, NCMP_S]), fs("vc_s", [P, DB, P])
            compress(nc, g)
            g.mixT = fs("mixT", [P, KC, T])
            pool_mixer(nc, g)
            attend_prompt(nc, g)
            attend_sample(nc, g)
            output(nc, g)
        g.x_hi, g.x_lo = sb("x_hi", [P, KC, T], F32R), sb("x_lo", [P, KC, T], F32R)
        with ExitStack() as middle:
            g.S = memory(nc, middle)[0]("scores", [P, NTT, 2 * PH, NKEY])
            queries(nc, g)
            retrieve(nc, g)
        experts(nc, g)


def kernel(**inputs):
    import concourse.bacc as bacc
    from concourse.bass_utils import run_bass_kernel_spmd

    arrays = prepare(inputs)
    nc = bacc.Bacc("TRN2", target_bir_lowering=False, num_devices=1)
    a = {n: nc.dram_tensor(n, v.shape, mybir.dt.from_np(v.dtype), kind="ExternalInput").ap() for n, v in arrays.items()}
    for n, (shape, dt) in OUTS.items():
        a[n] = nc.dram_tensor(n, shape, dt, kind="ExternalOutput").ap()
    a["gates_dense"] = nc.dram_tensor("gates_dense", (T // 32, P, NKEY * 32), F32, kind="Internal").ap()
    build(nc, a)
    res = run_bass_kernel_spmd(nc, [arrays], core_ids=[0]).results[0]
    r = {n: np.asarray(res[n]) for n in OUTS}

    y = r["out_y"].transpose(2, 1, 0).reshape(T, D)
    kv = r["out_kv"].reshape(KVH, HD, 3, 2, T).transpose(2, 4, 3, 0, 1)
    kvp = [kv[n, :SEQ].reshape(1, 1, SEQ, 2, KVH, HD) for n in range(3)]
    kvs = [kv[n, SEQ:].reshape(1, DB, DS, 2, KVH, HD) for n in range(3)]
    u = r["out_u"].transpose(2, 1, 0).reshape(PST + ST, 512)
    win_s = np.concatenate([r["out_win_past"].reshape(1, DB, WIN - DS, 2, KVH, HD), kvs[2]], 2)
    pool_s = np.concatenate([r["out_pool_past"].reshape(1, DB, PST - DS, 512), u[PST:].reshape(1, DB, DS, 512)], 2)
    return (y[:SEQ].reshape(1, SEQ, D), y[SEQ:].reshape(DB, DS, D), kvp[0], kvs[0], kvp[1], kvs[1], kvp[2], win_s,
            u[:PST].reshape(1, 1, PST, 512), pool_s)
```
